# Optimizing a Trainium2 kernel written in Bass

```python
import math
import jax, jax.numpy as jnp
from jax import lax
import numpy as np

D_MODEL = 1024
BATCH = 1
SEQ = 1024
DEPTH = 1

N_Q_HEADS = 8
N_KV_HEADS = 2
HEAD_DIM = 64
GQA_GROUP = N_Q_HEADS // N_KV_HEADS
ATTN_WIDTH = N_Q_HEADS * HEAD_DIM
KV_WIDTH = N_KV_HEADS * HEAD_DIM
WINDOW = 128
BLOCK = 128
N_BUCKETS = 32
MAX_DISTANCE = 128
POOL_WINDOWS = (2, 4, 8, 16)
N_POOL_GROUPS = len(POOL_WINDOWS)
POOL_WIDTH = D_MODEL // 2
POOL_GROUP_DIM = POOL_WIDTH // N_POOL_GROUPS
MIX_WIDTH = ATTN_WIDTH + POOL_WIDTH
IN_WIDTH = ATTN_WIDTH + 2 * KV_WIDTH + POOL_WIDTH
D_FF = 2816
MACARON_WEIGHT = 0.5
PLE_DIM = 256
EPS = 1e-6
NEG_INF = -1e30

kernel_name = "hybrid_swa_sink_pool_macaron_ple"

def rms_norm(x, gain):
    xf = x.astype(jnp.float32)
    y = xf * lax.rsqrt(jnp.mean(xf * xf, axis=-1, keepdims=True) + EPS)
    return (y * gain.astype(jnp.float32)).astype(x.dtype)

def swiglu(h, w_gu, w_down):
    g, u = jnp.split(h @ w_gu, 2, axis=-1)
    return (jax.nn.silu(g) * u) @ w_down

def t5_bucket(dist):
    n = jnp.maximum(dist, 0)
    max_exact = N_BUCKETS // 2
    nf = jnp.maximum(n, 1).astype(jnp.float32)
    large = max_exact + (jnp.log(nf / max_exact) / math.log(MAX_DISTANCE / max_exact)
                         * (N_BUCKETS - max_exact)).astype(jnp.int32)
    large = jnp.minimum(large, N_BUCKETS - 1)
    return jnp.where(n < max_exact, n, large)

def sliding_window_attention(q, k, v, rel_bias, sinks):
    B, S = q.shape[0], q.shape[1]
    nb = S // BLOCK
    q = q.reshape(B, nb, BLOCK, N_KV_HEADS, GQA_GROUP, HEAD_DIM)
    k = k.reshape(B, nb, BLOCK, N_KV_HEADS, HEAD_DIM)
    v = v.reshape(B, nb, BLOCK, N_KV_HEADS, HEAD_DIM)
    pad = ((0, 0), (1, 0), (0, 0), (0, 0), (0, 0))
    k_ctx = jnp.concatenate([jnp.pad(k, pad)[:, :-1], k], axis=2)
    v_ctx = jnp.concatenate([jnp.pad(v, pad)[:, :-1], v], axis=2)
    scores = jnp.einsum('bnqhgd,bnkhd->bnhgqk', q, k_ctx).astype(jnp.float32)
    scores = scores * (1.0 / math.sqrt(HEAD_DIM))
    qi = jnp.arange(BLOCK)[:, None]
    kj = jnp.arange(2 * BLOCK)[None, :]
    dist = qi + BLOCK - kj
    bias = rel_bias[t5_bucket(dist)]
    bias = jnp.transpose(bias, (2, 0, 1)).reshape(
        N_KV_HEADS, GQA_GROUP, BLOCK, 2 * BLOCK).astype(jnp.float32)
    key_pos = jnp.arange(nb)[:, None, None] * BLOCK - BLOCK + kj[None]
    valid = ((dist >= 0) & (dist < WINDOW))[None] & (key_pos >= 0)
    scores = jnp.where(valid[None, :, None, None], scores + bias, NEG_INF)
    sink = jnp.broadcast_to(
        sinks.astype(jnp.float32).reshape(N_KV_HEADS, GQA_GROUP)[None, None, :, :, None, None],
        scores.shape[:-1] + (1,))
    probs = jax.nn.softmax(jnp.concatenate([scores, sink], axis=-1), axis=-1)[..., :-1]
    out = jnp.einsum('bnhgqk,bnkhd->bnqhgd', probs.astype(v.dtype), v_ctx)
    return out.reshape(B, S, ATTN_WIDTH)

def multiscale_pool(u, pool_w, pool_scale):
    B, S, _ = u.shape
    uf = u.astype(jnp.float32)
    c = jnp.pad(jnp.cumsum(uf, axis=1), ((0, 0), (1, 0), (0, 0)))
    t = jnp.arange(S)
    means = []
    for g, w in enumerate(POOL_WINDOWS):
        cg = c[..., g * POOL_GROUP_DIM:(g + 1) * POOL_GROUP_DIM]
        lo = jnp.maximum(t + 1 - w, 0)
        s = cg[:, 1:] - jnp.take(cg, lo, axis=1)
        cnt = (t + 1 - lo).astype(jnp.float32)[None, :, None]
        means.append(s / cnt)
    mean = jnp.stack(means, axis=2)
    d = (mean - uf.reshape(B, S, N_POOL_GROUPS, POOL_GROUP_DIM)).astype(u.dtype)
    y = jnp.einsum('bsgc,gcd->bsgd', d, pool_w).reshape(B, S, POOL_WIDTH)
    return y * pool_scale

def setup_inputs(seed: int = 0) -> dict:
    key = jax.random.key(seed)
    ks = jax.random.split(key, 24)
    f32 = jnp.float32

    def nrm(k, shape, scale):
        return jax.random.normal(k, shape, f32) * scale

    def gain(k, shape):
        return 1.0 + 0.05 * jax.random.normal(k, shape, f32)

    L = DEPTH
    return {
        "x": nrm(ks[0], (BATCH, SEQ, D_MODEL), 1.0),
        "p": nrm(ks[1], (DEPTH, BATCH, SEQ, PLE_DIM), 1.0),
        "ffn1_norm": gain(ks[2], (L, D_MODEL)),
        "ffn1_w_gu": nrm(ks[3], (L, D_MODEL, 2 * D_FF), D_MODEL ** -0.5),
        "ffn1_w_down": nrm(ks[4], (L, D_FF, D_MODEL), D_FF ** -0.5),
        "mix_norm": gain(ks[5], (L, D_MODEL)),
        "w_in": nrm(ks[6], (L, D_MODEL, IN_WIDTH), D_MODEL ** -0.5),
        "q_norm": gain(ks[7], (L, HEAD_DIM)),
        "k_norm": gain(ks[8], (L, HEAD_DIM)),
        "rel_bias": nrm(ks[9], (N_BUCKETS, N_Q_HEADS), 0.5),
        "sinks": nrm(ks[10], (L, N_Q_HEADS), 1.0),
        "pool_w": nrm(ks[11], (L, N_POOL_GROUPS, POOL_GROUP_DIM, POOL_GROUP_DIM), POOL_GROUP_DIM ** -0.5),
        "pool_scale": gain(ks[12], (L, POOL_WIDTH)),
        "w_out": nrm(ks[13], (L, MIX_WIDTH, D_MODEL), MIX_WIDTH ** -0.5),
        "ffn2_norm": gain(ks[14], (L, D_MODEL)),
        "ffn2_w_gu": nrm(ks[15], (L, D_MODEL, 2 * D_FF), D_MODEL ** -0.5),
        "ffn2_w_down": nrm(ks[16], (L, D_FF, D_MODEL), D_FF ** -0.5),
        "ple_norm": gain(ks[17], (L, D_MODEL)),
        "ple_w_gate": nrm(ks[18], (L, D_MODEL, D_MODEL), D_MODEL ** -0.5),
        "ple_b_gate": nrm(ks[19], (L, D_MODEL), 0.02),
        "ple_w_proj": nrm(ks[20], (L, PLE_DIM, D_MODEL), PLE_DIM ** -0.5),
        "ple_post_norm": gain(ks[21], (L, D_MODEL)),
    }

def reference(x, p, ffn1_norm, ffn1_w_gu, ffn1_w_down, mix_norm, w_in, q_norm, k_norm,
              rel_bias, sinks, pool_w, pool_scale, w_out, ffn2_norm, ffn2_w_gu, ffn2_w_down,
              ple_norm, ple_w_gate, ple_b_gate, ple_w_proj, ple_post_norm):
    B, S, _ = x.shape
    for i in range(DEPTH):
        x = x + MACARON_WEIGHT * swiglu(rms_norm(x, ffn1_norm[i]), ffn1_w_gu[i], ffn1_w_down[i])
        h = rms_norm(x, mix_norm[i])
        proj = h @ w_in[i]
        q, k, v, u = jnp.split(
            proj, [ATTN_WIDTH, ATTN_WIDTH + KV_WIDTH, ATTN_WIDTH + 2 * KV_WIDTH], axis=-1)
        q = rms_norm(q.reshape(B, S, N_Q_HEADS, HEAD_DIM), q_norm[i])
        k = rms_norm(k.reshape(B, S, N_KV_HEADS, HEAD_DIM), k_norm[i])
        v = v.reshape(B, S, N_KV_HEADS, HEAD_DIM)
        a = sliding_window_attention(q, k, v, rel_bias, sinks[i])
        m = multiscale_pool(u, pool_w[i], pool_scale[i])
        x = x + jnp.concatenate([a, m], axis=-1) @ w_out[i]
        x = x + MACARON_WEIGHT * swiglu(rms_norm(x, ffn2_norm[i]), ffn2_w_gu[i], ffn2_w_down[i])
        gate = jax.nn.sigmoid(rms_norm(x, ple_norm[i]) @ ple_w_gate[i] + ple_b_gate[i])
        e = rms_norm(p[i] @ ple_w_proj[i], ple_post_norm[i])
        x = x + gate * e
    return x


_drawn_inputs = setup_inputs


def setup_inputs(seed=0):
    import zlib

    import numpy as np

    out = dict(_drawn_inputs(seed))
    spreads = {}
    factors = {'ffn1_norm': 2.8,
     'q_norm': 8.0,
     'k_norm': 8.0,
     'sinks': 178.351,
     'ffn2_norm': 3.611,
     'ple_norm': 25.298,
     'ple_b_gate': 62.304,
     'ple_post_norm': 9.432,
     'rel_bias': 3.211,
     'pool_scale': 4.248}
    for name, (base, spread) in spreads.items():
        noise = np.random.default_rng([zlib.crc32(name.encode()), seed]).standard_normal(out[name].shape)
        drawn = base * np.exp(spread * noise) if base else spread * noise
        out[name] = __import__('jax').numpy.asarray(drawn.astype(out[name].dtype))
    for name, factor in factors.items():
        out[name] = (out[name] * factor).astype(out[name].dtype)
    return out
```

```python
import math
from contextlib import ExitStack

import numpy as np

import concourse.bass as bass
from concourse import mybir

F32 = mybir.dt.float32
F32R = mybir.dt.float32r
ACT = mybir.ActivationFunctionType
ALU = mybir.AluOpType

P = 128
D_MODEL = 1024
SEQ = 1024
N_Q_HEADS = 8
N_KV_HEADS = 2
HEAD_DIM = 64
ATTN_WIDTH = N_Q_HEADS * HEAD_DIM
KV_WIDTH = N_KV_HEADS * HEAD_DIM
N_BUCKETS = 32
MAX_DISTANCE = 128
WINDOW = 128
POOL_WINDOWS = (2, 4, 8, 16)
POOL_WIDTH = D_MODEL // 2
D_FF = 2816
PLE_DIM = 256
MACARON_WEIGHT = 0.5
EPS = 1e-6
NEG_INF = -1e30

KT = D_MODEL // P
PT_TILES = PLE_DIM // P
HALF = SEQ // 2
NB = SEQ // P
HB = NB // 2
HPK = N_Q_HEADS // N_KV_HEADS
NG = len(POOL_WINDOWS)
HALO = max(POOL_WINDOWS)
FT = D_FF // P
GF = 2
GROUPS = FT // GF
UNIT = KT * P
SKEW = 3 * P

C_G = {"ffn1": 0, "mix": 8, "ffn2": 16, "ple": 24, "post": 32}
C_BGATE, C_PSCALE, C_QN, C_KN, C_SINK, C_EPS, C_EPSQ = 40, 48, 52, 53, 54, 62, 63
N_SMALL = 64
C_GAIN = [C_G["ffn1"], C_G["mix"], C_G["ffn2"], C_G["ple"]]
K_ID, K_ONES, K_BLK, K_RC = 0, P, 2 * P, 3 * P
N_CONST = K_RC + NG * HALO

W_PROJ, W_FFN1 = 0, 2
FFN_UNITS = 3 * FT
W_IN = W_FFN1 + FFN_UNITS
N_IN = 10
W_OUT = W_IN + N_IN
W_FFN2 = W_OUT + KT
W_GATE = W_FFN2 + FFN_UNITS
N_UNITS = W_GATE + KT
NRAW = 2
N_MIXU = 2 * N_IN + 2 * KT
S_P, S_PROJ, S_POOLW = 0, PT_TILES, PT_TILES + 2
S_FFN1 = S_POOLW + 1
S_MIX = S_FFN1 + FFN_UNITS
S_FFN2 = S_MIX + N_MIXU
S_GATE = S_FFN2 + FFN_UNITS
MIX_SLOTS = 2 * GF
DN_SLOT = 2 * GF

GU = 2 * FT
RES_FFN = 2 * KT * GROUPS
RES_MIX = 2 * KT

COL_Q, COL_K, COL_V, COL_U = 0, 4, 5, 6


def mix_plan():
    def win(a, what, i=0):
        return ("win", a, what, i)

    plan = [win(0, "k"), ("norm", 5), win(0, "v"), ("qks", 0, "k", 0)]
    plan += [win(0, "u", 0), ("vt", 0)] + [win(0, "u", g) for g in range(1, NG)]
    plan += [win(0, "q", 0)]
    for t in range(1, 4):
        plan += [win(0, "q", t), ("qks", 0, "q", t - 1)]
    fill = [win(1, "k"), win(1, "v")] + [win(1, "u", g) for g in range(NG)] + [win(1, "q", t) for t in range(3)]
    plan += [fill[0], ("qks", 0, "q", 3)]
    fill = fill[1:]
    more = {0: [("qks", 1, "k", 0)], 1: [("vt", 1)], 6: [("qks", 1, "q", 0)], 7: [("qks", 1, "q", 1)]}
    for u in range(8):
        plan.append(("scores", u))
        if u:
            plan.append(("pv", u - 1))
        if u < NG:
            plan.append(("prep", 0, u))
        plan.append(fill[u])
        plan.append(("probs", u))
        if 1 <= u <= NG:
            plan.append(("pool", 0, u - 1))
        plan += more.get(u, [])
    plan += [("pv", 7), win(1, "q", 3), ("qks", 1, "q", 2)]
    fill = [("wout", 0, d) for d in range(KT)]
    plan += [fill[0], ("qks", 1, "q", 3)]
    for u in range(8, 16):
        plan.append(("scores", u))
        if u > 8:
            plan.append(("pv", u - 1))
        if u - 8 < NG:
            plan.append(("prep", 1, u - 8))
        if u - 7 < KT:
            plan.append(fill[u - 7])
        plan.append(("probs", u))
        if 1 <= u - 8 <= NG:
            plan.append(("pool", 1, u - 9))
    plan += [("pv", 15), ("norm", 6)]
    plan += [("wout", 1, d) for d in range(KT)]
    plan += [("norm", 7)]
    return plan


PLAN = mix_plan()
WIN_ORDER = [[(s[2], s[3]) for s in PLAN if s[0] == "win" and s[1] == a] for a in (0, 1)]
assert WIN_ORDER[0][:1] == [("k", 0)] and all(len(x) == N_IN for x in WIN_ORDER)


def dram_unit(what, i):
    return W_IN + {"q": COL_Q, "k": COL_K, "v": COL_V, "u": COL_U}[what] + i


MAIN = [("proj", a, d) for a in (0, 1) for d in range(KT)]
MAIN += [s for s in PLAN if s[0] in ("win", "pool", "wout")]
MAIN += [("gate", a, d) for a in (0, 1) for d in range(KT)]
MAIN_AT = {s: n for n, s in enumerate(MAIN)}
MIXU = [s for s in PLAN if s[0] in ("win", "wout")]
MIXU_AT = {s: m for m, s in enumerate(MIXU)}
assert len(MIXU) == N_MIXU and N_MIXU % MIX_SLOTS == 0
N_GATE0 = MAIN_AT[("gate", 0, 0)]


def unit_of(step):
    return dram_unit(step[2], step[3]) if step[0] == "win" else W_OUT + step[2]


def freed_table():
    kinds = {"sq": 0, "act": 0, "lo": 0, "res": RES_FFN, "sig": 0}
    out = []
    for s in MAIN:
        if s[0] == "proj":
            k = "sq"
        elif s[0] == "win":
            k = "act"
        elif s[0] == "pool":
            k = "lo"
        elif s[0] == "wout":
            k = "res"
        else:
            k = "sig"
        kinds[k] += 1
        out.append((k, kinds[k]))
    return out


FREED = freed_table()

BANK7 = [("band", h) for h in range(N_Q_HEADS)] + [("norm", n) for n in range(4)]
BANK7 += [("norm", 4)] + [s for s in PLAN if s[0] in ("norm", "qks", "vt")] + [("norm", 8), ("norm", 9)]
BANK7_AT = {s: i for i, s in enumerate(BANK7)}
QKS = [s for s in PLAN if s[0] == "qks"]
QKS_AT = {s[1:]: i for i, s in enumerate(QKS)}
POOLS = [(a, g) for a in (0, 1) for g in range(NG)]


def program(nc, xT, pT, units, poolw, small, const, onehot, rel, band, e_dram, out):
    with ExitStack() as ctx:
        cursor = [-(-nc.sbuf_base // 64) * 64]

        def place(name, shape, dt=F32, at=None):
            size = 4 * int(np.prod(shape[1:]))
            where = cursor[0] if at is None else at
            if at is None:
                cursor[0] += -(-size // 32) * 32
            return nc.alloc_sbuf_tensor_at(name, list(shape), dt, offset=where), where

        x_sb, _ = place("x_sb", (P, KT, SEQ))
        h_hi, _ = place("h_hi", (P, KT, SEQ), F32R)
        h_lo, _ = place("h_lo", (P, KT, SEQ), F32R)
        w_hi, w_lo = [], []
        for s in range(3 * GF):
            if s == DN_SLOT:
                dn_at = cursor[0]
            w_hi.append(place(f"w_hi{s}", (P, UNIT), F32R)[0])
            w_lo.append(place(f"w_lo{s}", (P, UNIT), F32R)[0])
        dn_end = cursor[0]
        raw = [place(f"raw{i}", (P, UNIT))[0] for i in range(NRAW)]
        act_hi, act_at = place("act_hi", (P, GF, SEQ), F32R)
        act_lo, _ = place("act_lo", (P, GF, SEQ), F32R)
        work_at = cursor[0]
        silu = [place(f"silu{i}", (P, HALF))[0] for i in range(2)]
        prod = [place(f"prod{i}", (P, HALF))[0] for i in range(2)]
        acc = [place(f"acc{a}", (P, HALF))[0] for a in (0, 1)]
        sq = [place(f"sq{i}", (P, HALF))[0] for i in range(2)]
        rstd = [place(f"rstd{a}", (P, HALF))[0] for a in (0, 1)]
        hn = [place(f"hn{i}", (P, HALF))[0] for i in range(2)]
        bias, bias_at = place("bias", (P, N_Q_HEADS, 2 * P))
        pw_hi, _ = place("pw_hi", (P, NG * P), F32R)
        pw_lo, _ = place("pw_lo", (P, NG * P), F32R)
        small_sb, _ = place("small_sb", (P, N_SMALL))
        const_sb, _ = place("const_sb", (P, N_CONST))
        stats, _ = place("stats", (P, 6, HPK))
        rel_sb, _ = place("rel_sb", (N_BUCKETS + 1, N_Q_HEADS))
        tick, _ = place("tick", (P, 1))
        zero, _ = place("zero", (P, 1))
        k_sb, mix_at = place("k_sb", (P, SEQ))
        v_sb, _ = place("v_sb", (P, NB, P))
        d_hi, _ = place("d_hi", (P, HALF), F32R)
        d_lo, _ = place("d_lo", (P, HALF), F32R)
        qb = [place(f"qb{i}", (P, HALF))[0] for i in range(2)]
        assert cursor[0] <= nc.sbuf_usable_end, (cursor[0], nc.sbuf_usable_end)
        q_sb, _ = place("q_sb", (P, HPK, SEQ), at=act_at)
        probs, _ = place("probs", (P, HPK, 2 * P), at=work_at)
        probsT, _ = place("probsT", (P, 2, HPK * P), at=work_at + 8 * HALF)
        UB = HALO + HALF
        ub, _ = place("ub", (P, NG, UB), at=dn_at)
        win_a, _ = place("win_a", (P, UB), at=dn_at + 4 * NG * UB)
        win_b, _ = place("win_b", (P, UB), at=dn_at + 4 * (NG + 1) * UB)
        vT, _ = place("vT", (P, HALF), at=dn_at + 4 * (NG + 2) * UB)
        assert dn_at + 4 * (NG + 2) * UB + 4 * HALF <= dn_end
        oh_sb, _ = place("oh_sb", (N_BUCKETS + 1, SKEW), at=mix_at)
        relb, _ = place("relb", (N_BUCKETS + 1, N_Q_HEADS, P), at=mix_at + 4 * SKEW)
        gband = [place(f"gband{i}", (P, SKEW), at=mix_at + 4 * (SKEW + N_Q_HEADS * P + i * SKEW))[0]
                 for i in range(4)]
        e_sb = [place("e_a", (P, KT, HALF), at=mix_at)[0], place("e_b", (P, KT, HALF), at=act_at)[0]]
        re_sb, _ = place("re_sb", (P, 2, HALF), at=bias_at)
        et = silu + prod

        ident = const_sb[:, K_ID:K_ID + P]
        ones = const_sb[:, K_ONES:K_ONES + P]
        blockones = const_sb[:, K_BLK:K_BLK + P]
        NEGM, SM, ES, DEN, RCP, MX = range(6)

        def col(c):
            return small_sb[:, c:c + 1]

        def tok(a):
            return slice(a * HALF, (a + 1) * HALF)

        def plain(ap):
            return ap.bitcast(F32)

        bank = [ctx.enter_context(nc.psum_tensor(f"bank{i}", [P, 512], F32)) for i in range(8)]
        main_bank, gate_bank, up_bank, down_bank = bank[0:2], bank[0:2], bank[2:4], bank[4:7]
        score_bank, probsT_bank, pv_bank, sum_bank = bank[2:4], bank[4:6], bank[6], bank[7]

        def sem(name):
            return ctx.enter_context(nc.semaphore(name))

        small_in, const_in, oh_in, rel_in = sem("small_in"), sem("const_in"), sem("oh_in"), sem("rel_in")
        x_in = [sem(f"x_in{i}") for i in range(4)]
        raw_in = [sem(f"raw_in{i}") for i in range(NRAW)]
        unit_hi, unit_split = sem("unit_hi"), sem("unit_split")
        zero_made = sem("zero_made")
        rel_one, rel_spread, band_made, band_copied = sem("rel_one"), sem("rel_spread"), sem("band_made"), sem("band_copied")
        band_out = [sem(f"band_out{i}") for i in range(4)]
        bias_in = sem("bias_in")
        e_copied = sem("e_copied")
        e_out = [sem(f"e_out{i}") for i in range(4)]
        re_out = [sem(f"re_out{a}") for a in (0, 1)]
        e_in = [sem(f"e_in{a}") for a in (0, 1)]
        main_made, main_copied, sig_made = sem("main_made"), sem("main_copied"), sem("sig_made")
        gate_made, up_made, silu_made, product_made = sem("gate_made"), sem("up_made"), sem("silu_made"), sem("product_made")
        act_rounded, act_split = sem("act_rounded"), sem("act_split")
        down_made, res_added = sem("down_made"), sem("res_added")
        square_made, squares_added, sum_made = sem("square_made"), sem("squares_added"), sem("sum_made")
        std_made, rstd_made = sem("std_made"), sem("rstd_made")
        h_normed, h_rounded, h_split = sem("h_normed"), sem("h_rounded"), sem("h_split")
        qk_square, qk_sum, qk_std, qk_normed = sem("qk_square"), sem("qk_sum"), sem("qk_std"), sem("qk_normed")
        v_turned, v_copied = sem("v_turned"), sem("v_copied")
        pool_in, pool_rounded, pool_split = sem("pool_in"), sem("pool_rounded"), sem("pool_split")
        scores_made, scores_biased, max_made, exp_made = sem("scores_made"), sem("scores_biased"), sem("max_made"), sem("exp_made")
        probs_normed, probs_turned, probsT_copied = sem("probs_normed"), sem("probs_turned"), sem("probsT_copied")
        pv_made, attn_rounded, attn_split = sem("pv_made"), sem("attn_rounded"), sem("attn_split")
        dve_step = sem("dve_step")
        y_made, y_out = sem("y_made"), sem("y_out")

        freed_sem = {"sq": square_made, "act": main_copied, "lo": pool_split, "res": res_added, "sig": sig_made}
        assert FREED[MAIN_AT[PLAN[0]]][1] == 1

        def copied(step):
            kind, value = FREED[MAIN_AT[step]]
            assert kind == "act"
            return value

        def h_count(nrm, k):
            return KT * (nrm - 2) + k + 1

        def sq_count(nrm, k):
            return KT * nrm + k + 1

        def acc_count(nrm, k):
            return (KT - 1) * nrm + k

        block = ctx.enter_context(nc.Block())

        def store(sp, n):
            a, d = n // KT, n % KT
            sp.wait_ge(y_made, n + 1)
            sp.dma_start(out[d * P:(d + 1) * P, tok(a)], x_sb[:, d, tok(a)]).then_inc(y_out, 16)

        @block.sync
        def _(sp):
            def load(n, src, size=UNIT):
                if n >= NRAW:
                    sp.wait_ge(unit_split, n - NRAW + 1)
                sp.dma_start(raw[n % NRAW][:, 0:size], src).then_inc(raw_in[n % NRAW], 16)

            def ffn_loads(w0, s0, after):
                per = 3 * GF
                assert per % NRAW == 0
                for j in range(2 * GF):
                    load(s0 + j, units[w0 + j])
                with sp.Fori(0, GROUPS - 1) as g:
                    for j in range(per):
                        n = s0 + 2 * GF + j
                        sp.wait_ge(unit_split, g * per + (n - NRAW + 1))
                        src = units[bass.ds(g * per + (w0 + 2 * GF + j), 1), :, :].rearrange("a p n -> (a p) n")
                        sp.dma_start(raw[n % NRAW][:, :], src).then_inc(raw_in[n % NRAW], 16)
                for j in range(GF):
                    load(s0 + FFN_UNITS - GF + j, units[w0 + FFN_UNITS - GF + j])
                for j in range(2 * GF):
                    load(s0 + FFN_UNITS + j, units[after[j]])

            for k in range(PT_TILES):
                load(S_P + k, pT[k * P:(k + 1) * P, :])
            for j in range(2):
                load(S_PROJ + j, units[W_PROJ + j])
            load(S_POOLW, poolw, NG * P)
            ffn_loads(W_FFN1, S_FFN1, [unit_of(s) for s in MIXU[:MIX_SLOTS]])
            for m in range(MIX_SLOTS, N_MIXU):
                load(S_MIX + m, units[unit_of(MIXU[m])])
            for i in range(4):
                sp.wait_ge(e_out[i], 16 * (2 * KT // 4))
            for a in (0, 1):
                sp.wait_ge(re_out[a], 16)
            sp.wait_ge(pv_made, 2 * NB)
            sp.wait_ge(pool_split, 2 * NG)
            sp.wait_ge(qk_normed, len(QKS))
            sp.wait_ge(scores_biased, HPK * 2 * NB)
            sp.dma_start(e_sb[0][:, :, :], e_dram[0, :, 0:KT, :]).then_inc(e_in[0], 16)
            for a in (0, 1):
                sp.dma_start(re_sb[:, a, :], e_dram[a, :, KT, :]).then_inc(e_in[a], 16)
            ffn_loads(W_FFN2, S_FFN2, [W_GATE + j for j in range(MIX_SLOTS)])
            sp.wait_ge(down_made, 2 * RES_FFN)
            sp.dma_start(e_sb[1][:, :, :], e_dram[1, :, 0:KT, :]).then_inc(e_in[1], 16)
            for m in range(MIX_SLOTS, 2 * KT):
                load(S_GATE + m, units[W_GATE + m % KT])
                if m >= MIX_SLOTS + 4:
                    store(sp, m - MIX_SLOTS - 4)
            for n in range(2 * KT - MIX_SLOTS - 4, 2 * KT):
                store(sp, n)
            sp.wait_ge(y_out, 16 * 2 * KT)

        @block.gpsimd
        def _(pool):
            def split(raw_tile, hi, lo, rounded):
                pool.tensor_scalar(hi, raw_tile, 1.0, 1.0, ALU.mult, ALU.mult).then_inc(unit_hi, 1)
                pool.wait_ge(unit_hi, rounded)
                pool.tensor_tensor(lo, raw_tile, plain(hi), ALU.subtract).then_inc(unit_split, 1)

            def unit(n, hi, lo, size=UNIT):
                pool.wait_ge(raw_in[n % NRAW], 16 * (n // NRAW + 1))
                split(raw[n % NRAW][:, 0:size], hi, lo, n + 1)

            def slot_unit(n, s):
                unit(n, w_hi[s][:, :], w_lo[s][:, :])

            def ffn_units(ph, s0):
                per = 3 * GF
                with pool.Fori(0, GROUPS - 1) as g:
                    for j in range(per):
                        n = s0 + 2 * GF + j
                        if j < GF:
                            s, used, count = DN_SLOT + j, gate_made, g * (2 * GF) + (ph * GU + 1)
                        else:
                            s = j - GF
                            used, count = up_made, g * (2 * GF) + (ph * GU + GF + s // 2 + 1)
                        pool.wait_ge(used, count)
                        pool.wait_ge(raw_in[n % NRAW], g * (16 * per // NRAW) + 16 * (n // NRAW + 1))
                        pool.tensor_tensor(tick[:, :], zero[:, :], zero[:, :], ALU.add)
                        split(raw[n % NRAW][:, :], w_hi[s][:, :], w_lo[s][:, :], g * per + (n + 1))
                pool.wait_ge(gate_made, (ph + 1) * GU - 2 * GF + 1)
                for j in range(GF):
                    slot_unit(s0 + FFN_UNITS - GF + j, DN_SLOT + j)
                for s in range(MIX_SLOTS):
                    pool.wait_ge(up_made, (ph + 1) * GU - GF + s // 2 + 1)
                    slot_unit(s0 + FFN_UNITS + s, s)

            pool.memset(zero[:, :], 0.0).then_inc(zero_made, 1)
            pool.wait_ge(zero_made, 1)
            for k in range(PT_TILES):
                unit(S_P + k, act_hi[:, k, :], act_lo[:, k, :])
            for j in range(2):
                slot_unit(S_PROJ + j, DN_SLOT + j)
            unit(S_POOLW, pw_hi[:, :], pw_lo[:, :], NG * P)
            for s in range(2 * GF):
                slot_unit(S_FFN1 + s, s)
            pool.wait_ge(main_made, 2 * KT)
            ffn_units(0, S_FFN1)
            for m in range(MIX_SLOTS, N_MIXU):
                pool.wait_ge(main_made, MAIN_AT[MIXU[m - MIX_SLOTS]] + 1)
                slot_unit(S_MIX + m, m % MIX_SLOTS)
            for s in range(MIX_SLOTS):
                pool.wait_ge(main_made, MAIN_AT[MIXU[N_MIXU - MIX_SLOTS + s]] + 1)
                slot_unit(S_FFN2 + s, s)
            pool.wait_ge(pool_in, 2 * NG)
            pool.wait_ge(v_turned, 2)
            ffn_units(1, S_FFN2)
            for m in range(MIX_SLOTS, 2 * KT):
                pool.wait_ge(main_made, N_GATE0 + m - MIX_SLOTS + 1)
                slot_unit(S_GATE + m, m % MIX_SLOTS)

        @block.tensor
        def _(pe):
            def three(ps, whi, wlo, vhi, vlo, first, last):
                pe.matmul(ps, whi, vhi, start=first, stop=False)
                pe.matmul(ps, whi, vlo, start=False, stop=False)
                return pe.matmul(ps, wlo, vhi, start=False, stop=last)

            def wait_sum_bank(use):
                i = BANK7_AT[use]
                if i:
                    kind, *which = BANK7[i - 1]
                    done = {"band": band_copied, "norm": std_made, "qks": qk_std, "vt": v_copied}[kind]
                    pe.wait_ge(done, (QKS_AT[tuple(which)] if kind == "qks" else which[0]) + 1)

            def wait_main_bank(n):
                if n >= 2:
                    kind, value = FREED[n - 2]
                    pe.wait_ge(freed_sem[kind], value)

            def norm_sum(nrm):
                pe.wait_ge(squares_added, acc_count(nrm, KT - 1))
                wait_sum_bank(("norm", nrm))
                pe.matmul(sum_bank[:, :], ones, acc[nrm % 2][:, :], start=True, stop=True).then_inc(sum_made, 1)

            def eight(ps, s, a, nrm=None):
                for k in range(KT):
                    if nrm is not None:
                        pe.wait_ge(h_split, h_count(nrm, k))
                    c = slice(k * P, (k + 1) * P)
                    last = three(ps[:, :], w_hi[s][:, c], w_lo[s][:, c], h_hi[:, k, tok(a)], h_lo[:, k, tok(a)],
                                 k == 0, k == KT - 1)
                return last

            def ffn(ph, s0):
                per = 3 * GF

                def gate_up(g, i, nrm=None):
                    a, f = i // GF, i % GF
                    pe.wait_ge(h_split, h_count(4 * ph + 2 + a, KT - 1))
                    if i >= 2:
                        pe.wait_ge(product_made, g * (2 * GF) + (ph * GU + i - 1))
                    pe.wait_ge(unit_split, g * per + (s0 + 2 * f + 1))
                    eight(gate_bank[i % 2], 2 * f, a).then_inc(gate_made, 1)
                    if nrm is not None:
                        norm_sum(nrm)
                    pe.wait_ge(unit_split, g * per + (s0 + 2 * f + 2))
                    eight(up_bank[i % 2], 2 * f + 1, a).then_inc(up_made, 1)

                def down(g, a):
                    pe.wait_ge(act_split, g * (2 * GF) + (ph * GU + GF * (a + 1)))
                    pe.wait_ge(unit_split, g * per + (s0 + per))
                    r0 = ph * (RES_FFN + RES_MIX)
                    for d in range(KT):
                        r = a * KT + d
                        if r >= 3:
                            pe.wait_ge(res_added, g * (2 * KT) + (r0 + r - 2))
                        c = slice(d * P, (d + 1) * P)
                        for f in range(GF):
                            last = three(down_bank[r % 3][:, :], w_hi[DN_SLOT + f][:, c], w_lo[DN_SLOT + f][:, c],
                                         act_hi[:, f, tok(a)], act_lo[:, f, tok(a)], f == 0, f == GF - 1)
                        last.then_inc(down_made, 1)

                with pe.Fori(0, GROUPS - 1) as g:
                    for i in range(2 * GF):
                        gate_up(g, i)
                    for a in (0, 1):
                        down(g, a)
                g = GROUPS - 1
                for i in range(2 * GF - 1):
                    gate_up(g, i)
                down(g, 0)
                gate_up(g, 2 * GF - 1, nrm=4 * ph + 4)
                down(g, 1)

            pe.wait_ge(oh_in, 16)
            pe.wait_ge(const_in, 16)
            for h in range(N_Q_HEADS):
                pe.wait_ge(rel_spread, h + 1)
                wait_sum_bank(("band", h))
                pe.matmul(sum_bank[:, 0:SKEW], relb[:, h, :], oh_sb[:, :], start=True, stop=True).then_inc(band_made, 1)

            pe.wait_ge(unit_split, S_PROJ + 2)
            for a in (0, 1):
                for d in range(KT):
                    n = a * KT + d
                    wait_main_bank(n)
                    s, j = DN_SLOT + d // 4, d % 4
                    for k in range(PT_TILES):
                        c = slice((j * PT_TILES + k) * P, (j * PT_TILES + k + 1) * P)
                        last = three(main_bank[n % 2][:, :], w_hi[s][:, c], w_lo[s][:, c],
                                     act_hi[:, k, tok(a)], act_lo[:, k, tok(a)], k == 0, k == PT_TILES - 1)
                    last.then_inc(main_made, 1)
            for nrm in range(4):
                norm_sum(nrm)
            pe.wait_ge(square_made, sq_count(1, KT - 1))
            ffn(0, S_FFN1)

            pe.wait_ge(product_made, GU)
            seen = set()
            for step in PLAN:
                kind = step[0]
                if kind == "win":
                    n, m, a = MAIN_AT[step], MIXU_AT[step], step[1]
                    if n >= 2 * KT + 2:
                        wait_main_bank(n)
                    pe.wait_ge(unit_split, S_MIX + m + 1)
                    eight(main_bank[n % 2], m % MIX_SLOTS, a, None if a in seen else 4 + a).then_inc(main_made, 1)
                    seen.add(a)
                elif kind == "norm":
                    norm_sum(step[1])
                elif kind == "qks":
                    i = QKS_AT[step[1:]]
                    pe.wait_ge(qk_square, i + 1)
                    wait_sum_bank(step)
                    pe.matmul(sum_bank[:, :], blockones, qb[i % 2][:, :], start=True, stop=True).then_inc(qk_sum, 1)
                elif kind == "vt":
                    pe.wait_ge(main_copied, copied(("win", step[1], "v", 0)))
                    wait_sum_bank(step)
                    for j in range(HB):
                        c = slice(j * P, (j + 1) * P)
                        last = pe.transpose(sum_bank[:, c], vT[:, c], ident)
                    last.then_inc(v_turned, 1)
                elif kind == "scores":
                    u = step[1]
                    b, kv = u // 2, u % 2
                    p0, off = kv * HEAD_DIM, (P if b == 0 else 0)
                    pe.wait_ge(qk_normed, QKS_AT[(b // HB, "q", HPK - 1)] + 1)
                    if u:
                        pe.wait_ge(scores_biased, HPK * u)
                    for h in range(HPK):
                        c = (h % 2) * 2 * P
                        last = pe.matmul(score_bank[h // 2][:, c + off:c + 2 * P],
                                         q_sb[p0:p0 + HEAD_DIM, h, b * P:(b + 1) * P],
                                         k_sb[p0:p0 + HEAD_DIM, max(b - 1, 0) * P:(b + 1) * P], start=True, stop=True)
                    last.then_inc(scores_made, 1)
                elif kind == "probs":
                    u = step[1]
                    pe.wait_ge(probs_normed, HPK * (u + 1))
                    pe.wait_ge(res_added, RES_FFN)
                    if u:
                        pe.wait_ge(probsT_copied, u)
                    for kb in ((1,) if u < 2 else (0, 1)):
                        for h in range(HPK):
                            last = pe.transpose(probsT_bank[kb][:, h * P:(h + 1) * P],
                                                probs[:, h, kb * P:(kb + 1) * P], ident)
                    last.then_inc(probs_turned, 1)
                elif kind == "pv":
                    u = step[1]
                    b = u // 2
                    pe.wait_ge(probsT_copied, u + 1)
                    pe.wait_ge(v_copied, b // HB + 1)
                    if u:
                        pe.wait_ge(attn_split, u)
                    kbs = (1,) if b == 0 else (0, 1)
                    for kb in kbs:
                        last = pe.matmul(pv_bank[:, :], v_sb[:, b - 1 + kb, :], probsT[:, kb, :],
                                         start=kb == kbs[0], stop=kb == 1)
                    last.then_inc(pv_made, 1)
                elif kind == "pool":
                    n, g = MAIN_AT[step], step[2]
                    wait_main_bank(n)
                    pe.wait_ge(pool_in, POOLS.index(step[1:]) + 1)
                    c = slice(g * P, (g + 1) * P)
                    three(main_bank[n % 2][:, :], pw_hi[:, c], pw_lo[:, c], d_hi[:, :], d_lo[:, :],
                          True, True).then_inc(main_made, 1)
                elif kind == "wout":
                    n, m, a = MAIN_AT[step], MIXU_AT[step], step[1]
                    wait_main_bank(n)
                    pe.wait_ge(unit_split, S_MIX + m + 1)
                    pe.wait_ge(attn_split, NB * (a + 1))
                    pe.wait_ge(pool_split, NG * (a + 1))
                    eight(main_bank[n % 2], m % MIX_SLOTS, a).then_inc(main_made, 1)

            pe.wait_ge(res_added, RES_FFN + RES_MIX)
            ffn(1, S_FFN2)

            pe.wait_ge(product_made, 2 * GU)
            for a in (0, 1):
                for d in range(KT):
                    n, m = MAIN_AT[("gate", a, d)], a * KT + d
                    if m >= 2:
                        wait_main_bank(n)
                    pe.wait_ge(unit_split, S_GATE + m + 1)
                    eight(main_bank[n % 2], m % MIX_SLOTS, a, 8 + a if d == 0 else None).then_inc(main_made, 1)
                    if m == 0:
                        norm_sum(9)

        @block.scalar
        def _(act):
            def square(nrm, k, src):
                dst = acc[nrm % 2] if k == 0 else sq[k % 2]
                if k == 0:
                    if nrm >= 2:
                        act.wait_ge(sum_made, nrm - 1)
                elif k <= 2:
                    if nrm >= 1:
                        act.wait_ge(squares_added, acc_count(nrm, 0))
                else:
                    act.wait_ge(squares_added, acc_count(nrm, k - 2))
                act.activation(dst[:, :], src, ACT.Square).then_inc(square_made, 1)

            def std(nrm):
                act.wait_ge(sum_made, nrm + 1)
                if nrm >= 4:
                    act.wait_ge(h_normed, h_count(nrm - 2, KT - 1))
                elif nrm >= 2:
                    act.wait_ge(re_out[nrm % 2], 16)
                act.activation(rstd[nrm % 2][:, :], sum_bank[:, :], ACT.Sqrt, bias=col(C_EPS),
                               scale=1.0 / D_MODEL).then_inc(std_made, 1)

            def round_h(nrm, k):
                act.wait_ge(h_normed, h_count(nrm, k))
                act.activation(h_hi[:, k, tok(nrm % 2)], hn[k % 2][:, :], ACT.Copy).then_inc(h_rounded, 1)

            def ffn(ph):
                def silu_tile(g, i):
                    act.wait_ge(gate_made, g * (2 * GF) + (ph * GU + i + 1))
                    act.activation(silu[i % 2][:, :], gate_bank[i % 2][:, :], ACT.Silu).then_inc(silu_made, 1)

                def round_tile(g, i):
                    act.wait_ge(product_made, g * (2 * GF) + (ph * GU + i + 1))
                    act.activation(act_hi[:, i % GF, tok(i // GF)], prod[i % 2][:, :], ACT.Copy).then_inc(act_rounded, 1)

                with act.Fori(0, GROUPS - 1) as g:
                    for i in range(2 * GF):
                        silu_tile(g, i)
                        round_tile(g, i)
                g = GROUPS - 1
                r0 = ph * (RES_FFN + RES_MIX) + 2 * KT * g
                for i in range(2 * GF - 1):
                    silu_tile(g, i)
                    round_tile(g, i)
                for k in range(KT):
                    act.wait_ge(res_added, r0 + k + 1)
                    square(4 * ph + 4, k, x_sb[:, k, tok(0)])
                silu_tile(g, 2 * GF - 1)
                std(4 * ph + 4)
                round_tile(g, 2 * GF - 1)
                for k in range(KT):
                    round_h(4 * ph + 4, k)
                    act.wait_ge(res_added, r0 + KT + k + 1)
                    square(4 * ph + 5, k, x_sb[:, k, tok(1)])

            act.dma_start(const_sb[:, :], const).then_inc(const_in, 16)
            act.dma_start(small_sb[:, :], small).then_inc(small_in, 16)
            act.dma_start(oh_sb[:, :], onehot).then_inc(oh_in, 16)
            act.dma_start(rel_sb[0:N_BUCKETS, :], rel).then_inc(rel_in, 16)
            for i in range(4):
                a, k = i // 2, (i % 2) * (KT // 2)
                act.dma_start(x_sb[:, k:k + KT // 2, tok(a)],
                              xT[k * P:(k + KT // 2) * P, tok(a)].rearrange("(k p) t -> p k t", p=P)).then_inc(x_in[i], 16)

            for h in range(N_Q_HEADS):
                act.wait_ge(band_made, h + 1)
                if h >= 4:
                    act.wait_ge(band_out[h % 4], 16)
                act.activation(gband[h % 4][:, :], sum_bank[:, 0:SKEW], ACT.Copy).then_inc(band_copied, 1)
                act.wait_ge(band_copied, h + 1)
                act.dma_start(band[h], gband[h % 4][:, :]).then_inc(band_out[h % 4], 16)

            act.wait_ge(small_in, 16)
            for a in (0, 1):
                for d in range(KT):
                    n = a * KT + d
                    act.wait_ge(main_made, n + 1)
                    if n >= 4:
                        act.wait_ge(e_out[n % 4], 16 * (n // 4))
                    act.activation(et[n % 4][:, :], main_bank[n % 2][:, :], ACT.Copy).then_inc(e_copied, 1)
                    square(a, d, main_bank[n % 2][:, :])
                    act.wait_ge(e_copied, n + 1)
                    act.dma_start(e_dram[a, :, d, :], et[n % 4][:, :]).then_inc(e_out[n % 4], 16)
            for i in range(4):
                act.wait_ge(band_out[i], 32)
            skewed = bass.AP(tensor=band.tensor, offset=P - 1, ap=[[SKEW - 1, P], [P * SKEW, N_Q_HEADS], [1, 2 * P]])
            act.dma_start(bias[:, :, :], skewed).then_inc(bias_in, 16)
            for a in (0, 1):
                std(a)
                act.wait_ge(rstd_made, a + 1)
                act.dma_start(e_dram[a, :, KT, :], rstd[a][:, :]).then_inc(re_out[a], 16)
            for nrm in (2, 3):
                for k in range(KT):
                    act.wait_ge(x_in[2 * (nrm - 2) + k // (KT // 2)], 16)
                    square(nrm, k, x_sb[:, k, tok(nrm % 2)])
                std(nrm)
                for k in range(KT):
                    round_h(nrm, k)
            ffn(0)

            for step in PLAN:
                kind = step[0]
                if kind == "win":
                    n, a, what, i = MAIN_AT[step], *step[1:]
                    ps = main_bank[n % 2][:, :]
                    act.wait_ge(main_made, n + 1)
                    if what == "v":
                        if a:
                            act.wait_ge(v_turned, a)
                        act.activation(vT[:, :], ps, ACT.Copy).then_inc(main_copied, 1)
                    elif what == "u":
                        if a:
                            act.wait_ge(pool_in, i + 1)
                        act.activation(ub[:, i, HALO:UB], ps, ACT.Copy).then_inc(main_copied, 1)
                    else:
                        dst = k_sb[:, tok(a)] if what == "k" else q_sb[:, i, tok(a)]
                        j = QKS_AT[(a, what, i)]
                        act.activation(dst, ps, ACT.Copy).then_inc(main_copied, 1)
                        act.wait_ge(main_copied, copied(step))
                        if j >= 2:
                            act.wait_ge(qk_normed, j - 1)
                        act.activation(qb[j % 2][:, :], dst, ACT.Square).then_inc(qk_square, 1)
                elif kind == "qks":
                    i, q = QKS_AT[step[1:]], step[2] == "q"
                    act.wait_ge(qk_sum, i + 1)
                    act.activation(qb[i % 2][:, :], sum_bank[:, :], ACT.Sqrt, bias=col(C_EPSQ if q else C_EPS),
                                   scale=1.0 if q else 1.0 / HEAD_DIM).then_inc(qk_std, 1)
                elif kind == "vt":
                    a = step[1]
                    act.wait_ge(v_turned, a + 1)
                    act.activation(v_sb[:, a * HB:(a + 1) * HB, :], sum_bank[:, :].rearrange("p (b c) -> p b c", b=HB),
                                   ACT.Copy).then_inc(v_copied, 1)
                elif kind == "norm" and step[1] == 5:
                    std(5)
                    for k in range(KT):
                        round_h(5, k)
                elif kind == "norm":
                    std(step[1])
                    for k in range(KT):
                        round_h(step[1], k)
                elif kind == "scores":
                    u = step[1]
                    off = P if u < 2 else 0
                    act.wait_ge(max_made, u + 1)
                    act.activation(stats[:, ES, :], stats[:, SM, :], ACT.Exp)
                    for h in range(HPK):
                        last = act.activation(probs[:, h, off:], probs[:, h, off:], ACT.Exp, bias=stats[:, NEGM, h:h + 1],
                                              accum_out=stats[:, DEN, h:h + 1])
                    last.then_inc(exp_made, 1)
                elif kind == "probs":
                    u = step[1]
                    act.wait_ge(probs_turned, u + 1)
                    if u:
                        act.wait_ge(pv_made, u)
                    for kb in ((1,) if u < 2 else (0, 1)):
                        last = act.activation(probsT[:, kb, :], probsT_bank[kb][:, :], ACT.Copy)
                    last.then_inc(probsT_copied, 1)
                elif kind == "pv":
                    u = step[1]
                    b, p0 = u // 2, (u % 2) * HEAD_DIM
                    act.wait_ge(pv_made, u + 1)
                    act.activation(h_hi[p0:p0 + HEAD_DIM, 0:HPK, b * P:(b + 1) * P],
                                   pv_bank[p0:p0 + HEAD_DIM, :].rearrange("p (h q) -> p h q", h=HPK),
                                   ACT.Copy).then_inc(attn_rounded, 1)
                elif kind == "pool":
                    n, a, g = MAIN_AT[step], *step[1:]
                    act.wait_ge(main_made, n + 1)
                    act.activation(h_hi[:, HPK + g, tok(a)], main_bank[n % 2][:, :], ACT.Copy,
                                   scale=col(C_PSCALE + g)).then_inc(pool_rounded, 1)
                elif kind == "wout":
                    a, d = step[1:]
                    act.wait_ge(res_added, RES_FFN + a * KT + d + 1)
                    square(6 + a, d, x_sb[:, d, tok(a)])
            ffn(1)

            for a in (0, 1):
                for d in range(KT):
                    n, m = MAIN_AT[("gate", a, d)], a * KT + d
                    act.wait_ge(main_made, n + 1)
                    if m >= 2:
                        act.wait_ge(y_made, m - 1)
                    act.activation(silu[m % 2][:, :], main_bank[n % 2][:, :], ACT.Sigmoid,
                                   bias=col(C_BGATE + d)).then_inc(sig_made, 1)
                    if m == 0:
                        std(9)
                        for k in range(KT):
                            round_h(9, k)

        @block.vector
        def _(dve):
            steps = [0]

            def link(ins):
                steps[0] += 1
                ins.then_inc(dve_step, 1)
                dve.wait_ge(dve_step, steps[0])

            def accumulate(nrm, k):
                dve.wait_ge(square_made, sq_count(nrm, k))
                if k >= 2:
                    dve.wait_ge(squares_added, acc_count(nrm, k - 1))
                a = acc[nrm % 2][:, :]
                dve.tensor_tensor(a, a, sq[k % 2][:, :], ALU.add).then_inc(squares_added, 1)

            def reciprocal(nrm):
                r = rstd[nrm % 2][:, :]
                dve.wait_ge(std_made, nrm + 1)
                dve.reciprocal(r, r).then_inc(rstd_made, 1)
                dve.wait_ge(rstd_made, nrm + 1)

            def norm_tile(nrm, k):
                if h_count(nrm, k) > 2:
                    dve.wait_ge(h_split, h_count(nrm, k) - 2)
                g = C_GAIN[nrm // 2 - 1] + k
                dve.scalar_tensor_tensor(hn[k % 2][:, :], x_sb[:, k, tok(nrm % 2)], col(g), rstd[nrm % 2][:, :],
                                         ALU.mult, ALU.mult).then_inc(h_normed, 1)

            def split_tile(nrm, k):
                dve.wait_ge(h_rounded, h_count(nrm, k))
                a = tok(nrm % 2)
                dve.tensor_tensor(h_lo[:, k, a], hn[k % 2][:, :], plain(h_hi[:, k, a]), ALU.subtract).then_inc(h_split, 1)

            def norm_tiles(nrm):
                for k in range(KT):
                    norm_tile(nrm, k)
                    if k:
                        split_tile(nrm, k - 1)
                split_tile(nrm, KT - 1)

            def ffn(ph):
                def product(g, i):
                    t = ph * GU + i + 1
                    dve.wait_ge(up_made, g * (2 * GF) + t)
                    dve.wait_ge(silu_made, g * (2 * GF) + t)
                    if i >= 2:
                        dve.wait_ge(act_split, g * (2 * GF) + t - 2)
                    dve.tensor_tensor(prod[i % 2][:, :], silu[i % 2][:, :], up_bank[i % 2][:, :], ALU.mult).then_inc(product_made, 1)
                    dve.wait_ge(act_rounded, g * (2 * GF) + t)
                    f, a = i % GF, tok(i // GF)
                    dve.tensor_tensor(act_lo[:, f, a], prod[i % 2][:, :], plain(act_hi[:, f, a]), ALU.subtract).then_inc(act_split, 1)

                def residual(g, r):
                    dve.wait_ge(down_made, g * (2 * KT) + (ph * RES_FFN + r + 1))
                    x = x_sb[:, r % KT, tok(r // KT)]
                    dve.scalar_tensor_tensor(x, down_bank[r % 3][:, :], MACARON_WEIGHT, x, ALU.mult, ALU.add).then_inc(res_added, 1)

                with dve.Fori(0, GROUPS - 1) as g:
                    for i in range(2 * GF):
                        product(g, i)
                    for r in range(2 * KT):
                        residual(g, r)
                g, na, nb = GROUPS - 1, 4 * ph + 4, 4 * ph + 5
                for i in range(2 * GF - 1):
                    product(g, i)
                for k in range(KT):
                    residual(g, k)
                    if k >= 2:
                        accumulate(na, k - 1)
                accumulate(na, KT - 1)
                reciprocal(na)
                norm_tile(na, 0)
                product(g, 2 * GF - 1)
                for k in range(KT):
                    residual(g, KT + k)
                    if k + 1 < KT:
                        norm_tile(na, k + 1)
                    split_tile(na, k)
                    if k >= 2:
                        accumulate(nb, k - 1)
                accumulate(nb, KT - 1)

            dve.memset(rel_sb[N_BUCKETS:N_BUCKETS + 1, :], 1.0).then_inc(rel_one, 1)
            dve.wait_ge(rel_one, 1)
            dve.wait_ge(rel_in, 16)
            dve.wait_ge(const_in, 16)
            for h in range(N_Q_HEADS):
                dve.tensor_scalar(relb[:, h, :], const_sb[0:N_BUCKETS + 1, K_ONES:K_ONES + P], rel_sb[:, h:h + 1], None,
                                  ALU.mult).then_inc(rel_spread, 1)
            dve.wait_ge(small_in, 16)
            for nrm in (0, 1):
                for k in range(1, KT):
                    accumulate(nrm, k)
            for nrm in (0, 1):
                reciprocal(nrm)
            for nrm in (2, 3):
                for k in range(1, KT):
                    accumulate(nrm, k)
                reciprocal(nrm)
                norm_tiles(nrm)
            ffn(0)

            link(dve.memset(ub[:, :, 0:HALO], 0.0))
            dve.wait_ge(bias_in, 16)
            for step in PLAN:
                kind = step[0]
                if kind == "norm":
                    nrm = step[1]
                    if nrm > 5:
                        accumulate(nrm, KT - 1)
                    reciprocal(nrm)
                    norm_tiles(nrm)
                elif kind == "qks":
                    a, what, i = step[1:]
                    j = QKS_AT[step[1:]]
                    dve.wait_ge(qk_std, j + 1)
                    link(dve.reciprocal(qb[j % 2][:, :], qb[j % 2][:, :]))
                    t = k_sb[:, tok(a)] if what == "k" else q_sb[:, i, tok(a)]
                    dve.scalar_tensor_tensor(t, t, col(C_KN if what == "k" else C_QN), qb[j % 2][:, :],
                                             ALU.mult, ALU.mult).then_inc(qk_normed, 1)
                elif kind == "scores":
                    u = step[1]
                    kv, off = u % 2, (P if u < 2 else 0)
                    dve.wait_ge(scores_made, u + 1)
                    for h in range(HPK):
                        c = (h % 2) * 2 * P
                        hh = kv * HPK + h
                        dve.tensor_tensor_reduce(probs[:, h, off:], score_bank[h // 2][:, c + off:c + 2 * P],
                                                 bias[:, hh, off:], 1.0, col(C_SINK + hh), ALU.add, ALU.max,
                                                 stats[:, MX, h:h + 1]).then_inc(scores_biased, 1)
                    dve.wait_ge(scores_biased, HPK * (u + 1))
                    link(dve.tensor_scalar(stats[:, NEGM, :], stats[:, MX, :], -1.0, None, ALU.mult))
                    c = C_SINK + kv * HPK
                    dve.tensor_tensor(stats[:, SM, :], stats[:, NEGM, :], small_sb[:, c:c + HPK], ALU.add).then_inc(max_made, 1)
                    dve.wait_ge(exp_made, u + 1)
                    link(dve.tensor_tensor(stats[:, RCP, :], stats[:, DEN, :], stats[:, ES, :], ALU.add))
                    link(dve.reciprocal(stats[:, RCP, :], stats[:, RCP, :]))
                    for h in range(HPK):
                        dve.tensor_scalar(probs[:, h, off:], probs[:, h, off:], stats[:, RCP, h:h + 1], None,
                                          ALU.mult).then_inc(probs_normed, 1)
                elif kind == "pv":
                    u = step[1]
                    b, p0 = u // 2, (u % 2) * HEAD_DIM
                    at = (slice(p0, p0 + HEAD_DIM), slice(0, HPK), slice(b * P, (b + 1) * P))
                    dve.wait_ge(attn_rounded, u + 1)
                    dve.tensor_tensor(h_lo[at], pv_bank[p0:p0 + HEAD_DIM, :].rearrange("p (h q) -> p h q", h=HPK),
                                      plain(h_hi[at]), ALU.subtract).then_inc(attn_split, 1)
                elif kind == "prep":
                    a, g = step[1:]
                    u, w, i = ub[:, g, :], POOL_WINDOWS[g], POOLS.index((a, g))
                    if i:
                        dve.wait_ge(pool_in, i)
                    dve.wait_ge(main_copied, copied(("win", a, "u", g)))
                    s, reach = u, 1
                    bufs = [win_a, win_b]
                    while reach < w:
                        dst = bufs[0][:, :]
                        bufs.reverse()
                        lo = 2 * reach - 1
                        link(dve.tensor_tensor(dst[:, lo:UB], s[:, lo:UB], s[:, lo - reach:UB - reach], ALU.add))
                        s, reach = dst, 2 * reach
                    body = slice(2 * HALO, UB) if a == 0 else slice(HALO, UB)
                    ins = dve.scalar_tensor_tensor(s[:, body], s[:, body], 1.0 / w, u[:, body], ALU.mult, ALU.subtract)
                    if a == 0:
                        first = slice(HALO, 2 * HALO)
                        link(ins)
                        c = K_RC + g * HALO
                        link(dve.tensor_tensor(s[:, first], s[:, first], const_sb[:, c:c + HALO], ALU.mult))
                        ins = dve.tensor_tensor(s[:, first], s[:, first], u[:, first], ALU.subtract)
                    link(ins)
                    if i:
                        dve.wait_ge(main_made, MAIN_AT[("pool", *POOLS[i - 1])] + 1)
                    link(dve.tensor_copy(d_hi[:, :], s[:, HALO:UB]))
                    link(dve.tensor_tensor(d_lo[:, :], s[:, HALO:UB], plain(d_hi[:, :]), ALU.subtract))
                    dve.tensor_copy(u[:, 0:HALO], u[:, HALF:UB]).then_inc(pool_in, 1)
                elif kind == "pool":
                    n, a, g = MAIN_AT[step], *step[1:]
                    dve.wait_ge(pool_rounded, POOLS.index((a, g)) + 1)
                    dve.scalar_tensor_tensor(h_lo[:, HPK + g, tok(a)], main_bank[n % 2][:, :], col(C_PSCALE + g),
                                             plain(h_hi[:, HPK + g, tok(a)]), ALU.mult, ALU.subtract).then_inc(pool_split, 1)
                elif kind == "wout":
                    n, a, d = MAIN_AT[step], *step[1:]
                    if d == 0:
                        dve.wait_ge(res_added, RES_FFN + a * KT)
                    dve.wait_ge(main_made, n + 1)
                    x = x_sb[:, d, tok(a)]
                    dve.tensor_tensor(x, x, main_bank[n % 2][:, :], ALU.add).then_inc(res_added, 1)
                    if d >= 2:
                        accumulate(6 + a, d - 1)
            ffn(1)

            def finish(m):
                a, d = m // KT, m % KT
                e = e_sb[a][:, d, :]
                x = x_sb[:, d, tok(a)]
                dve.wait_ge(e_in[a], 32)
                link(dve.scalar_tensor_tensor(e, e, col(C_G["post"] + d), re_sb[:, a, :], ALU.mult, ALU.mult))
                dve.wait_ge(sig_made, m + 1)
                link(dve.tensor_tensor(e, e, silu[m % 2][:, :], ALU.mult))
                dve.tensor_tensor(x, x, e, ALU.add).then_inc(y_made, 1)

            for m in range(2 * KT):
                finish(m)
                if m == 0:
                    reciprocal(9)
                    norm_tiles(9)


def build(nc, xT, pT, units, poolw, small, const, onehot, rel, out):
    band = nc.dram_tensor("band", (N_Q_HEADS, P, SKEW), F32, kind="Internal").ap()
    e_dram = nc.dram_tensor("e_dram", (2, P, KT + 1, HALF), F32, kind="Internal").ap()
    program(nc, xT, pT, units, poolw, small, const, onehot, rel, band, e_dram, out)


def constants():
    c = np.zeros((P, N_CONST), np.float32)
    c[:, K_ID:K_ID + P] = np.eye(P)
    c[:, K_ONES:K_ONES + P] = 1.0
    c[:, K_BLK:K_BLK + P] = np.kron(np.eye(P // HEAD_DIM), np.ones((HEAD_DIM, HEAD_DIM)))
    for g, w in enumerate(POOL_WINDOWS):
        c[:, K_RC + g * HALO:K_RC + (g + 1) * HALO] = 1.0 / np.minimum(np.arange(HALO) + 1, w)
    return c


def onehots():
    oh = np.zeros((N_BUCKETS + 1, SKEW), np.float32)
    half = N_BUCKETS // 2
    for i in range(SKEW):
        n = 2 * P - 1 - i
        if 0 <= n < WINDOW:
            b = n if n < half else min(N_BUCKETS - 1, half + int(
                math.log(n / half) / math.log(MAX_DISTANCE / half) * (N_BUCKETS - half) + 1e-9))
            oh[b, i] = 1.0
        else:
            oh[N_BUCKETS, i] = NEG_INF
    return oh


def pack_ffn(w_gu, w_down):
    gu = w_gu.reshape(KT, P, 2, GROUPS, GF, P).transpose(3, 4, 2, 1, 0, 5).reshape(GROUPS, 2 * GF, P, UNIT)
    dn = w_down.reshape(GROUPS, GF, P, D_MODEL)
    return np.concatenate([gu, dn], axis=1).reshape(FFN_UNITS, P, UNIT)


def pack_square(w):
    n = w.shape[1] // P
    return w.reshape(KT, P, n, P).transpose(2, 1, 0, 3).reshape(n, P, UNIT)


def kernel(x, p, ffn1_norm, ffn1_w_gu, ffn1_w_down, mix_norm, w_in, q_norm, k_norm,
           rel_bias, sinks, pool_w, pool_scale, w_out, ffn2_norm, ffn2_w_gu, ffn2_w_down,
           ple_norm, ple_w_gate, ple_b_gate, ple_w_proj, ple_post_norm):
    import concourse.bacc as bacc
    from concourse.bass_utils import run_bass_kernel_spmd

    f = np.ascontiguousarray
    heads = np.arange(ATTN_WIDTH).reshape(N_KV_HEADS, HPK, HEAD_DIM).transpose(1, 0, 2).reshape(-1)
    w_in = np.asarray(w_in)[0]
    w_in = np.concatenate([w_in[:, heads], w_in[:, ATTN_WIDTH:]], axis=1)
    w_out = np.asarray(w_out)[0]
    w_out = np.concatenate([w_out[heads], w_out[ATTN_WIDTH:]], axis=0)
    proj = np.asarray(ple_w_proj)[0].reshape(PT_TILES, P, 2, KT // 2, P).transpose(2, 1, 3, 0, 4).reshape(2, P, UNIT)
    units = np.concatenate([
        proj, pack_ffn(np.asarray(ffn1_w_gu)[0], np.asarray(ffn1_w_down)[0]), pack_square(w_in), pack_square(w_out),
        pack_ffn(np.asarray(ffn2_w_gu)[0], np.asarray(ffn2_w_down)[0]), pack_square(np.asarray(ple_w_gate)[0])])

    def by_partition(v):
        return np.asarray(v)[0].reshape(-1, P).T

    def twice(v):
        return np.tile(np.asarray(v)[0], P // HEAD_DIM)[:, None]

    eps = np.zeros((P, 2), np.float32)
    eps[:, 0], eps[:, 1] = EPS, EPS * HEAD_DIM
    small = np.concatenate([
        by_partition(ffn1_norm), by_partition(mix_norm), by_partition(ffn2_norm), by_partition(ple_norm),
        by_partition(ple_post_norm), by_partition(ple_b_gate), by_partition(pool_scale), twice(q_norm), twice(k_norm),
        np.broadcast_to(np.asarray(sinks), (P, N_Q_HEADS)), eps], axis=1)
    arrays = {
        "xT": f(np.asarray(x)[0].T), "pT": f(np.asarray(p)[0, 0].T), "units": f(units),
        "poolw": f(np.asarray(pool_w)[0].transpose(1, 0, 2).reshape(P, NG * P)), "small": f(small),
        "const": constants(), "onehot": onehots(), "rel": f(np.asarray(rel_bias)),
    }
    nc = bacc.Bacc("TRN2", target_bir_lowering=False, num_devices=1, dynamic_dma_scratch_size=1024)
    args = [nc.dram_tensor(f"in_{k}", v.shape, mybir.dt.from_np(v.dtype), kind="ExternalInput").ap()
            for k, v in arrays.items()]
    out = nc.dram_tensor("outT", (D_MODEL, SEQ), F32, kind="ExternalOutput").ap()
    build(nc, *args, out)
    r = run_bass_kernel_spmd(nc, [{f"in_{k}": v for k, v in arrays.items()}], core_ids=[0])
    return f(r.results[0]["outT"].T)[None]
```

```python
import math
from contextlib import ExitStack

import numpy as np

import concourse.bass as bass
from concourse import mybir

F32 = mybir.dt.float32
F32R = mybir.dt.float32r
ACT = mybir.ActivationFunctionType
ALU = mybir.AluOpType

P = 128
D_MODEL = 1024
SEQ = 1024
N_Q_HEADS = 8
N_KV_HEADS = 2
HEAD_DIM = 64
ATTN_WIDTH = N_Q_HEADS * HEAD_DIM
KV_WIDTH = N_KV_HEADS * HEAD_DIM
N_BUCKETS = 32
MAX_DISTANCE = 128
WINDOW = 128
POOL_WINDOWS = (2, 4, 8, 16)
POOL_WIDTH = D_MODEL // 2
D_FF = 2816
PLE_DIM = 256
MACARON_WEIGHT = 0.5
EPS = 1e-6
NEG_INF = -1e30

KT = D_MODEL // P
PT_TILES = PLE_DIM // P
HALF = SEQ // 2
NB = SEQ // P
HB = NB // 2
HPK = N_Q_HEADS // N_KV_HEADS
NG = len(POOL_WINDOWS)
HALO = max(POOL_WINDOWS)
FT = D_FF // P
GF = 2
GROUPS = FT // GF
UNIT = KT * P
SKEW = 3 * P

C_G = {"ffn1": 0, "mix": 8, "ffn2": 16, "ple": 24, "post": 32}
C_BGATE, C_PSCALE, C_QN, C_KN, C_SINK, C_EPS, C_EPSQ = 40, 48, 52, 53, 54, 62, 63
N_SMALL = 64
C_GAIN = [C_G["ffn1"], C_G["mix"], C_G["ffn2"], C_G["ple"]]
K_ID, K_ONES, K_BLK, K_RC = 0, P, 2 * P, 3 * P
N_CONST = K_RC + NG * HALO

W_PROJ, W_FFN1 = 0, 2
FFN_UNITS = 3 * FT
W_IN = W_FFN1 + FFN_UNITS
N_IN = 10
W_OUT = W_IN + N_IN
W_FFN2 = W_OUT + KT
W_GATE = W_FFN2 + FFN_UNITS
N_UNITS = W_GATE + KT
NRAW = 2
N_MIXU = 2 * N_IN + 2 * KT
S_PROJ, S_POOLW = 0, 2
S_FFN1 = S_POOLW + 1
S_MIX = S_FFN1 + FFN_UNITS
S_FFN2 = S_MIX + N_MIXU
S_GATE = S_FFN2 + FFN_UNITS
MIX_SLOTS = 2 * GF
DN_SLOT = 2 * GF

GU = 2 * FT
RES_FFN = 2 * KT * GROUPS
RES_MIX = 2 * KT

COL_Q, COL_K, COL_V, COL_U = 0, 4, 5, 6


def mix_plan():
    def win(a, what, i=0):
        return ("win", a, what, i)

    plan = [win(0, "k"), ("norm", 3), win(0, "v"), ("qks", 0, "k", 0), win(0, "q", 0), ("vt", 0)]
    order = [win(0, "q", t) for t in range(1, HPK)] + [win(0, "u", g) for g in range(NG)] + [win(1, "k")]
    for j, step in enumerate(order):
        plan.append(step)
        if j < HPK:
            plan.append(("qks", 0, "q", j))
        plan += [("tile", 3, k) for k in range(2 * j, 2 * j + 2) if k <= KT]
    fill = [win(1, "v")] + [win(1, "q", t) for t in range(HPK)] + [win(1, "u", g) for g in range(NG - 1)]
    ready = {0: [("qks", 1, "k", 0)], 1: [("vt", 1)], 2: [("qks", 1, "q", 0)], 3: [("qks", 1, "q", 1)],
             4: [("qks", 1, "q", 2)], 5: [("qks", 1, "q", 3)]}
    for u in range(NB):
        plan.append(("scores", u))
        plan += ready.get(u, [])
        if u < NG:
            plan.append(("prep", 0, u))
        plan.append(fill[u])
        if u:
            plan.append(("pv", u - 1))
        plan.append(("probs", u))
        if 1 <= u <= NG:
            plan.append(("pool", 0, u - 1))
    plan += [win(1, "u", NG - 1), ("pv", NB - 1)]
    for u in range(NB, 2 * NB):
        plan.append(("scores", u))
        if u - NB < NG:
            plan.append(("prep", 1, u - NB))
        plan.append(("wout", 0, u - NB))
        if u > NB:
            plan.append(("pv", u - 1))
        plan.append(("probs", u))
        if 1 <= u - NB <= NG:
            plan.append(("pool", 1, u - NB - 1))
    plan += [("norm", 4), ("pv", 2 * NB - 1)]
    for d in range(KT):
        plan.append(("wout", 1, d))
        plan += [("tile", 4, k) for k in range(2 * d, 2 * d + 2) if k <= KT]
    plan += [("norm", 5)] + [("tile", 5, k) for k in range(KT + 1)]
    return plan


PLAN = mix_plan()
WIN_ORDER = [[(s[2], s[3]) for s in PLAN if s[0] == "win" and s[1] == a] for a in (0, 1)]
assert all(len(x) == N_IN for x in WIN_ORDER)


def dram_unit(what, i):
    return W_IN + {"q": COL_Q, "k": COL_K, "v": COL_V, "u": COL_U}[what] + i


MAIN = [("proj", a, d) for a in (0, 1) for d in range(KT)]
MAIN += [s for s in PLAN if s[0] in ("win", "pool", "wout")]
MAIN += [("gate", a, d) for a in (0, 1) for d in range(KT)]
MAIN_AT = {s: n for n, s in enumerate(MAIN)}
MIXU = [s for s in PLAN if s[0] in ("win", "wout")]
MIXU_AT = {s: m for m, s in enumerate(MIXU)}
assert len(MIXU) == N_MIXU and N_MIXU % MIX_SLOTS == 0
N_GATE0 = MAIN_AT[("gate", 0, 0)]


def unit_of(step):
    return dram_unit(step[2], step[3]) if step[0] == "win" else W_OUT + step[2]


def freed_table():
    kinds = {"esq": 0, "act": 0, "lo": 0, "res": RES_FFN, "sig": 0}
    out = []
    for s in MAIN:
        if s[0] == "proj":
            k = "esq"
        elif s[0] == "win":
            k = "act"
        elif s[0] == "pool":
            k = "lo"
        elif s[0] == "wout":
            k = "res"
        else:
            k = "sig"
        kinds[k] += 1
        out.append((k, kinds[k]))
    return out


FREED = freed_table()

BANK7 = [("norm", 0), ("norm", 1), ("e", 0), ("e", 1), ("norm", 2)]
BANK7 += [s for s in PLAN if s[0] in ("norm", "qks", "vt")] + [("norm", 6), ("norm", 7)]
BANK7_AT = {s: i for i, s in enumerate(BANK7)}
QKS = [s for s in PLAN if s[0] == "qks"]
QKS_AT = {s[1:]: i for i, s in enumerate(QKS)}
POOLS = [(a, g) for a in (0, 1) for g in range(NG)]


def program(nc, xT, pT, units, poolw, small, const, onehot, rel, band, e_dram, out):
    with ExitStack() as ctx:
        cursor = [-(-nc.sbuf_base // 64) * 64]

        def place(name, shape, dt=F32, at=None):
            size = 4 * int(np.prod(shape[1:]))
            where = cursor[0] if at is None else at
            if at is None:
                cursor[0] += -(-size // 32) * 32
            return nc.alloc_sbuf_tensor_at(name, list(shape), dt, offset=where), where

        x_sb, _ = place("x_sb", (P, KT, SEQ))
        h_hi, _ = place("h_hi", (P, KT, SEQ), F32R)
        h_lo, _ = place("h_lo", (P, KT, SEQ), F32R)
        w_hi, w_lo = [], []
        for s in range(3 * GF):
            if s == DN_SLOT:
                dn_at = cursor[0]
            w_hi.append(place(f"w_hi{s}", (P, UNIT), F32R)[0])
            w_lo.append(place(f"w_lo{s}", (P, UNIT), F32R)[0])
        dn_end = cursor[0]
        raw = [place(f"raw{i}", (P, UNIT))[0] for i in range(NRAW)]
        act_hi, act_at = place("act_hi", (P, GF, SEQ), F32R)
        act_lo, _ = place("act_lo", (P, GF, SEQ), F32R)
        work_at = cursor[0]
        silu = [place(f"silu{i}", (P, HALF))[0] for i in range(2)]
        prod = [place(f"prod{i}", (P, HALF))[0] for i in range(2)]
        acc = [place(f"acc{a}", (P, HALF))[0] for a in (0, 1)]
        sq = [place(f"sq{i}", (P, HALF))[0] for i in range(2)]
        rstd = [place(f"rstd{a}", (P, HALF))[0] for a in (0, 1)]
        hn = [place(f"hn{i}", (P, HALF))[0] for i in range(2)]
        bias, bias_at = place("bias", (P, N_Q_HEADS, 2 * P))
        pw_hi, _ = place("pw_hi", (P, NG * P), F32R)
        pw_lo, _ = place("pw_lo", (P, NG * P), F32R)
        small_sb, _ = place("small_sb", (P, N_SMALL))
        const_sb, _ = place("const_sb", (P, N_CONST))
        stats, _ = place("stats", (P, 6, HPK))
        rel_sb, _ = place("rel_sb", (N_BUCKETS + 1, N_Q_HEADS))
        tick, _ = place("tick", (P, 1))
        zero, _ = place("zero", (P, 1))
        k_sb, mix_at = place("k_sb", (P, SEQ))
        v_sb, _ = place("v_sb", (P, NB, P))
        d_hi, _ = place("d_hi", (P, HALF), F32R)
        d_lo, _ = place("d_lo", (P, HALF), F32R)
        qb = [place(f"qb{i}", (P, HALF))[0] for i in range(2)]
        assert cursor[0] <= nc.sbuf_usable_end, (cursor[0], nc.sbuf_usable_end)
        q_sb, _ = place("q_sb", (P, HPK, SEQ), at=act_at)
        probs, _ = place("probs", (P, HPK, 2 * P), at=work_at)
        probsT, _ = place("probsT", (P, 2, HPK * P), at=work_at + 8 * HALF)
        UB = HALO + HALF
        ub, _ = place("ub", (P, NG, UB), at=dn_at)
        win_a, _ = place("win_a", (P, UB), at=dn_at + 4 * NG * UB)
        win_b, _ = place("win_b", (P, UB), at=dn_at + 4 * (NG + 1) * UB)
        vT, _ = place("vT", (P, HALF), at=dn_at + 4 * (NG + 2) * UB)
        assert dn_at + 4 * (NG + 2) * UB + 4 * HALF <= dn_end
        oh_sb, _ = place("oh_sb", (N_BUCKETS + 1, SKEW), at=mix_at)
        relb, _ = place("relb", (N_BUCKETS + 1, N_Q_HEADS, P), at=mix_at + 4 * SKEW)
        gband_at = mix_at + 4 * (SKEW + N_Q_HEADS * P)
        gband = [place(f"gband{i}", (P, SKEW), at=gband_at + 4 * i * SKEW)[0] for i in range(4)]
        eacc_at = gband_at + 16 * SKEW
        eacc = [place(f"eacc{a}", (P, HALF), at=eacc_at + 4 * a * HALF)[0] for a in (0, 1)]
        assert eacc_at + 8 * HALF <= cursor[0]
        p_raw, _ = place("p_raw", (P, PT_TILES, SEQ), at=bias_at)
        esq = [place(f"esq{i}", (P, HALF), at=bias_at + 4 * i * HALF)[0] for i in range(2)]
        e_sb = [place("e_a", (P, KT, HALF), at=mix_at)[0], place("e_b", (P, KT, HALF), at=act_at)[0]]
        re_sb, _ = place("re_sb", (P, 2, HALF), at=bias_at)
        et = silu + prod

        ident = const_sb[:, K_ID:K_ID + P]
        ones = const_sb[:, K_ONES:K_ONES + P]
        blockones = const_sb[:, K_BLK:K_BLK + P]
        NEGM, SM, ES, DEN, RCP, MX = range(6)

        def col(c):
            return small_sb[:, c:c + 1]

        def tok(a):
            return slice(a * HALF, (a + 1) * HALF)

        def plain(ap):
            return ap.bitcast(F32)

        bank = [ctx.enter_context(nc.psum_tensor(f"bank{i}", [P, 512], F32)) for i in range(8)]
        main_bank, gate_bank, up_bank, down_bank = bank[0:2], bank[0:2], bank[2:4], bank[4:7]
        band_bank = bank[2:6]
        score_bank, probsT_bank, pv_bank, sum_bank = bank[2:4], bank[4:6], bank[6], bank[7]

        def sem(name):
            return ctx.enter_context(nc.semaphore(name))

        small_in, const_in, oh_in, rel_in = sem("small_in"), sem("const_in"), sem("oh_in"), sem("rel_in")
        x_in = [sem(f"x_in{i}") for i in range(4)]
        raw_in = [sem(f"raw_in{i}") for i in range(NRAW)]
        unit_hi, unit_split = sem("unit_hi"), sem("unit_split")
        zero_made = sem("zero_made")
        p_in, p_rounded, p_split = sem("p_in"), sem("p_rounded"), sem("p_split")
        e_square, e_added, e_sum, e_std, e_rstd = (sem(n) for n in ("e_square", "e_added", "e_sum", "e_std", "e_rstd"))
        rel_one, rel_spread, band_made, band_copied = sem("rel_one"), sem("rel_spread"), sem("band_made"), sem("band_copied")
        band_out = [sem(f"band_out{i}") for i in range(4)]
        bias_in = sem("bias_in")
        e_copied = sem("e_copied")
        e_out = [sem(f"e_out{i}") for i in range(4)]
        re_out = [sem(f"re_out{a}") for a in (0, 1)]
        e_in = [sem(f"e_in{a}") for a in (0, 1)]
        main_made, main_copied, sig_made = sem("main_made"), sem("main_copied"), sem("sig_made")
        gate_made, up_made, silu_made, product_made = sem("gate_made"), sem("up_made"), sem("silu_made"), sem("product_made")
        act_rounded, act_split = sem("act_rounded"), sem("act_split")
        down_made, res_added = sem("down_made"), sem("res_added")
        square_made, squares_added, sum_made = sem("square_made"), sem("squares_added"), sem("sum_made")
        std_made, rstd_made = sem("std_made"), sem("rstd_made")
        h_normed, h_rounded, h_split = sem("h_normed"), sem("h_rounded"), sem("h_split")
        qk_square, qk_sum, qk_std, qk_normed = sem("qk_square"), sem("qk_sum"), sem("qk_std"), sem("qk_normed")
        v_turned, v_copied = sem("v_turned"), sem("v_copied")
        pool_in, pool_rounded, pool_split = sem("pool_in"), sem("pool_rounded"), sem("pool_split")
        scores_made, scores_biased, max_made, exp_made = sem("scores_made"), sem("scores_biased"), sem("max_made"), sem("exp_made")
        probs_normed, probs_turned, probsT_copied = sem("probs_normed"), sem("probs_turned"), sem("probsT_copied")
        pv_made, attn_rounded, attn_split = sem("pv_made"), sem("attn_rounded"), sem("attn_split")
        dve_step = sem("dve_step")
        y_made, y_out = sem("y_made"), sem("y_out")

        freed_sem = {"esq": e_square, "act": main_copied, "lo": pool_split, "res": res_added, "sig": sig_made}
        assert FREED[MAIN_AT[PLAN[0]]][1] == 1

        def copied(step):
            kind, value = FREED[MAIN_AT[step]]
            assert kind == "act"
            return value

        def h_count(nrm, k):
            return KT * nrm + k + 1

        def sq_count(nrm, k):
            return KT * nrm + k + 1

        def acc_count(nrm, k):
            return (KT - 1) * nrm + k

        block = ctx.enter_context(nc.Block())

        def store(sp, n):
            a, d = n // KT, n % KT
            sp.wait_ge(y_made, n + 1)
            sp.dma_start(out[d * P:(d + 1) * P, tok(a)], x_sb[:, d, tok(a)]).then_inc(y_out, 16)

        @block.sync
        def _(sp):
            def load(n, src, size=UNIT):
                if n >= NRAW:
                    sp.wait_ge(unit_split, n - NRAW + 1)
                sp.dma_start(raw[n % NRAW][:, 0:size], src).then_inc(raw_in[n % NRAW], 16)

            def ffn_loads(w0, s0, after):
                per = 3 * GF
                assert per % NRAW == 0
                for j in range(2 * GF):
                    load(s0 + j, units[w0 + j])
                with sp.Fori(0, GROUPS - 1) as g:
                    for j in range(per):
                        n = s0 + 2 * GF + j
                        sp.wait_ge(unit_split, g * per + (n - NRAW + 1))
                        src = units[bass.ds(g * per + (w0 + 2 * GF + j), 1), :, :].rearrange("a p n -> (a p) n")
                        sp.dma_start(raw[n % NRAW][:, :], src).then_inc(raw_in[n % NRAW], 16)
                for j in range(GF):
                    load(s0 + FFN_UNITS - GF + j, units[w0 + FFN_UNITS - GF + j])
                for j in range(2 * GF):
                    load(s0 + FFN_UNITS + j, units[after[j]])

            sp.dma_start(p_raw[:, :, :], pT.rearrange("(k p) t -> p k t", p=P)).then_inc(p_in, 16)
            for j in range(2):
                load(S_PROJ + j, units[W_PROJ + j])
            for h in range(N_Q_HEADS):
                sp.wait_ge(band_copied, h + 1)
                sp.dma_start(band[h], gband[h % 4][:, :]).then_inc(band_out[h % 4], 16)
            load(S_POOLW, poolw, NG * P)
            ffn_loads(W_FFN1, S_FFN1, [unit_of(s) for s in MIXU[:MIX_SLOTS]])
            for m in range(MIX_SLOTS, N_MIXU):
                load(S_MIX + m, units[unit_of(MIXU[m])])
            for i in range(4):
                sp.wait_ge(e_out[i], 16 * (2 * KT // 4))
            for a in (0, 1):
                sp.wait_ge(re_out[a], 16)
            sp.wait_ge(pv_made, 2 * NB)
            sp.wait_ge(pool_split, 2 * NG)
            sp.wait_ge(qk_normed, len(QKS))
            sp.wait_ge(scores_biased, HPK * 2 * NB)
            sp.dma_start(e_sb[0][:, :, :], e_dram[0, :, 0:KT, :]).then_inc(e_in[0], 16)
            for a in (0, 1):
                sp.dma_start(re_sb[:, a, :], e_dram[a, :, KT, :]).then_inc(e_in[a], 16)
            ffn_loads(W_FFN2, S_FFN2, [W_GATE + j for j in range(MIX_SLOTS)])
            sp.wait_ge(down_made, 2 * RES_FFN)
            sp.dma_start(e_sb[1][:, :, :], e_dram[1, :, 0:KT, :]).then_inc(e_in[1], 16)
            for m in range(MIX_SLOTS, 2 * KT):
                load(S_GATE + m, units[W_GATE + m % KT])
                if m >= MIX_SLOTS + 4:
                    store(sp, m - MIX_SLOTS - 4)
            for n in range(2 * KT - MIX_SLOTS - 4, 2 * KT):
                store(sp, n)
            sp.wait_ge(y_out, 16 * 2 * KT)

        @block.gpsimd
        def _(pool):
            def split(raw_tile, hi, lo, rounded):
                pool.tensor_scalar(hi, raw_tile, 1.0, 1.0, ALU.mult, ALU.mult).then_inc(unit_hi, 1)
                pool.wait_ge(unit_hi, rounded)
                pool.tensor_tensor(lo, raw_tile, plain(hi), ALU.subtract).then_inc(unit_split, 1)

            def unit(n, hi, lo, size=UNIT):
                pool.wait_ge(raw_in[n % NRAW], 16 * (n // NRAW + 1))
                split(raw[n % NRAW][:, 0:size], hi, lo, n + 1)

            def slot_unit(n, s):
                unit(n, w_hi[s][:, :], w_lo[s][:, :])

            def ffn_units(ph, s0):
                per = 3 * GF
                with pool.Fori(0, GROUPS - 1) as g:
                    for j in range(per):
                        n = s0 + 2 * GF + j
                        if j < GF:
                            s, used, count = DN_SLOT + j, gate_made, g * (2 * GF) + (ph * GU + 1)
                        else:
                            s = j - GF
                            used, count = up_made, g * (2 * GF) + (ph * GU + GF + s // 2 + 1)
                        pool.wait_ge(used, count)
                        pool.wait_ge(raw_in[n % NRAW], g * (16 * per // NRAW) + 16 * (n // NRAW + 1))
                        pool.tensor_tensor(tick[:, :], zero[:, :], zero[:, :], ALU.add)
                        split(raw[n % NRAW][:, :], w_hi[s][:, :], w_lo[s][:, :], g * per + (n + 1))
                pool.wait_ge(gate_made, (ph + 1) * GU - 2 * GF + 1)
                for j in range(GF):
                    slot_unit(s0 + FFN_UNITS - GF + j, DN_SLOT + j)
                for s in range(MIX_SLOTS):
                    if s == 2:
                        a = acc[1][:, :]
                        for k in range(1, KT):
                            pool.wait_ge(square_made, sq_count(4 * ph + 3, k))
                            if k >= 2:
                                pool.wait_ge(squares_added, acc_count(4 * ph + 3, k - 1))
                            pool.tensor_tensor(a, a, sq[k % 2][:, :], ALU.add).then_inc(squares_added, 1)
                    pool.wait_ge(up_made, (ph + 1) * GU - GF + s // 2 + 1)
                    slot_unit(s0 + FFN_UNITS + s, s)

            pool.memset(zero[:, :], 0.0).then_inc(zero_made, 1)
            pool.wait_ge(zero_made, 1)
            for j in range(2):
                slot_unit(S_PROJ + j, DN_SLOT + j)
            unit(S_POOLW, pw_hi[:, :], pw_lo[:, :], NG * P)
            for s in range(2 * GF):
                slot_unit(S_FFN1 + s, s)
            pool.wait_ge(main_made, 2 * KT)
            ffn_units(0, S_FFN1)
            for m in range(MIX_SLOTS, N_MIXU):
                pool.wait_ge(main_made, MAIN_AT[MIXU[m - MIX_SLOTS]] + 1)
                slot_unit(S_MIX + m, m % MIX_SLOTS)
            for s in range(MIX_SLOTS):
                pool.wait_ge(main_made, MAIN_AT[MIXU[N_MIXU - MIX_SLOTS + s]] + 1)
                slot_unit(S_FFN2 + s, s)
            pool.wait_ge(pool_in, 2 * NG)
            pool.wait_ge(v_turned, 2)
            ffn_units(1, S_FFN2)
            for m in range(MIX_SLOTS, 2 * KT):
                pool.wait_ge(main_made, N_GATE0 + m - MIX_SLOTS + 1)
                slot_unit(S_GATE + m, m % MIX_SLOTS)

        @block.tensor
        def _(pe):
            def three(ps, whi, wlo, vhi, vlo, first, last):
                pe.matmul(ps, whi, vhi, start=first, stop=False)
                pe.matmul(ps, whi, vlo, start=False, stop=False)
                return pe.matmul(ps, wlo, vhi, start=False, stop=last)

            def wait_sum_bank(use):
                i = BANK7_AT[use]
                if i:
                    kind, *which = BANK7[i - 1]
                    done = {"e": e_std, "norm": std_made, "qks": qk_std, "vt": v_copied}[kind]
                    pe.wait_ge(done, (QKS_AT[tuple(which)] if kind == "qks" else which[0]) + 1)

            def wait_main_bank(n):
                if n >= 2:
                    kind, value = FREED[n - 2]
                    pe.wait_ge(freed_sem[kind], value)

            def norm_sum(nrm):
                pe.wait_ge(squares_added, acc_count(nrm, KT - 1))
                wait_sum_bank(("norm", nrm))
                pe.matmul(sum_bank[:, :], ones, acc[nrm % 2][:, :], start=True, stop=True).then_inc(sum_made, 1)

            def eight(ps, s, a, nrm=None, order=range(KT), ahead=None):
                for k in order:
                    if nrm is not None:
                        pe.wait_ge(h_split, h_count(nrm, k))
                    if ahead and k == 0:
                        ahead()
                    c = slice(k * P, (k + 1) * P)
                    last = three(ps[:, :], w_hi[s][:, c], w_lo[s][:, c], h_hi[:, k, tok(a)], h_lo[:, k, tok(a)],
                                 k == order[0], k == order[-1])
                return last

            def ffn(ph, s0):
                per = 3 * GF

                def gate_up(g, i, between=None):
                    a, f = i // GF, i % GF
                    pe.wait_ge(h_split, h_count(4 * ph + a, KT - 1))
                    if i >= 2:
                        pe.wait_ge(product_made, g * (2 * GF) + (ph * GU + i - 1))
                    pe.wait_ge(unit_split, g * per + (s0 + 2 * f + 1))
                    eight(gate_bank[i % 2], 2 * f, a).then_inc(gate_made, 1)
                    if between:
                        between()
                    pe.wait_ge(unit_split, g * per + (s0 + 2 * f + 2))
                    eight(up_bank[i % 2], 2 * f + 1, a).then_inc(up_made, 1)

                def down_tiles(g, a, tiles, fs):
                    for d in tiles:
                        r = a * KT + d
                        if r >= 3 and fs[0] == 0:
                            pe.wait_ge(res_added, g * (2 * KT) + (ph * (RES_FFN + RES_MIX) + r - 2))
                        c = slice(d * P, (d + 1) * P)
                        for f in fs:
                            last = three(down_bank[r % 3][:, :], w_hi[DN_SLOT + f][:, c], w_lo[DN_SLOT + f][:, c],
                                         act_hi[:, f, tok(a)], act_lo[:, f, tok(a)], f == 0, f == GF - 1)
                        if fs[-1] == GF - 1:
                            last.then_inc(down_made, 1)

                def down(g, a):
                    pe.wait_ge(act_split, g * (2 * GF) + (ph * GU + GF * (a + 1)))
                    pe.wait_ge(unit_split, g * per + (s0 + per))
                    down_tiles(g, a, range(KT), range(GF))

                with pe.Fori(0, GROUPS - 1) as g:
                    for i in range(2 * GF):
                        gate_up(g, i)
                    for a in (0, 1):
                        down(g, a)
                g = GROUPS - 1
                for i in range(2 * GF - 1):
                    gate_up(g, i)
                down(g, 0)
                gate_up(g, 2 * GF - 1, between=lambda: norm_sum(4 * ph + 2))
                assert GF == 2
                down_tiles(g, 1, range(3), (0,))
                pe.wait_ge(act_split, (ph + 1) * GU)
                down_tiles(g, 1, range(3), (1,))
                down_tiles(g, 1, range(3, KT), range(GF))

            pe.wait_ge(oh_in, 16)
            pe.wait_ge(const_in, 16)
            for h in range(N_Q_HEADS):
                pe.wait_ge(rel_spread, h + 1)
                if h >= len(band_bank):
                    pe.wait_ge(band_copied, h - len(band_bank) + 1)
                pe.matmul(band_bank[h % len(band_bank)][:, 0:SKEW], relb[:, h, :], oh_sb[:, :], start=True, stop=True).then_inc(band_made, 1)

            pe.wait_ge(p_split, PT_TILES)
            for a in (0, 1):
                for d in range(KT):
                    n = a * KT + d
                    pe.wait_ge(unit_split, S_PROJ + d // 4 + 1)
                    wait_main_bank(n)
                    s, j = DN_SLOT + d // 4, d % 4
                    for k in range(PT_TILES):
                        c = slice((j * PT_TILES + k) * P, (j * PT_TILES + k + 1) * P)
                        last = three(main_bank[n % 2][:, :], w_hi[s][:, c], w_lo[s][:, c],
                                     act_hi[:, k, tok(a)], act_lo[:, k, tok(a)], k == 0, k == PT_TILES - 1)
                    last.then_inc(main_made, 1)
                norm_sum(a)
            for a in (0, 1):
                pe.wait_ge(e_added, (KT - 1) * (a + 1))
                wait_sum_bank(("e", a))
                pe.matmul(sum_bank[:, :], ones, eacc[a][:, :], start=True, stop=True).then_inc(e_sum, 1)
            pe.wait_ge(e_square, 2 * KT)
            pe.wait_ge(band_copied, N_Q_HEADS)
            ffn(0, S_FFN1)

            def pv(u):
                b = u // 2
                pe.wait_ge(probsT_copied, u + 1)
                pe.wait_ge(v_copied, b // HB + 1)
                if u:
                    pe.wait_ge(attn_split, u)
                kbs = (1,) if b == 0 else (0, 1)
                for kb in kbs:
                    last = pe.matmul(pv_bank[:, :], v_sb[:, b - 1 + kb, :], probsT[:, kb, :],
                                     start=kb == kbs[0], stop=kb == 1)
                last.then_inc(pv_made, 1)

            pe.wait_ge(product_made, GU)
            seen = set()
            for step in PLAN:
                kind = step[0]
                if kind == "win":
                    n, m, a = MAIN_AT[step], MIXU_AT[step], step[1]
                    if n >= 2 * KT + 2:
                        wait_main_bank(n)
                    pe.wait_ge(unit_split, S_MIX + m + 1)
                    eight(main_bank[n % 2], m % MIX_SLOTS, a, None if a in seen else 2 + a).then_inc(main_made, 1)
                    seen.add(a)
                elif kind == "norm":
                    norm_sum(step[1])
                elif kind == "qks":
                    i = QKS_AT[step[1:]]
                    pe.wait_ge(qk_square, i + 1)
                    wait_sum_bank(step)
                    pe.matmul(sum_bank[:, :], blockones, qb[i % 2][:, :], start=True, stop=True).then_inc(qk_sum, 1)
                elif kind == "vt":
                    pe.wait_ge(main_copied, copied(("win", step[1], "v", 0)))
                    wait_sum_bank(step)
                    for j in range(HB):
                        c = slice(j * P, (j + 1) * P)
                        last = pe.transpose(sum_bank[:, c], vT[:, c], ident)
                    last.then_inc(v_turned, 1)
                elif kind == "scores":
                    u = step[1]
                    b, kv = u // 2, u % 2
                    p0, off = kv * HEAD_DIM, (P if b == 0 else 0)
                    pe.wait_ge(qk_normed, QKS_AT[(b // HB, "q", HPK - 1)] + 1)
                    if u:
                        pe.wait_ge(scores_biased, HPK * u)
                    for h in range(HPK):
                        c = (h % 2) * 2 * P
                        last = pe.matmul(score_bank[h // 2][:, c + off:c + 2 * P],
                                         q_sb[p0:p0 + HEAD_DIM, h, b * P:(b + 1) * P],
                                         k_sb[p0:p0 + HEAD_DIM, max(b - 1, 0) * P:(b + 1) * P], start=True, stop=True)
                    last.then_inc(scores_made, 1)
                elif kind == "probs":
                    u = step[1]
                    pe.wait_ge(probs_normed, HPK * (u + 1))
                    pe.wait_ge(res_added, RES_FFN)
                    if u:
                        pe.wait_ge(probsT_copied, u)
                    for kb in ((1,) if u < 2 else (0, 1)):
                        for h in range(HPK):
                            last = pe.transpose(probsT_bank[kb][:, h * P:(h + 1) * P],
                                                probs[:, h, kb * P:(kb + 1) * P], ident)
                    last.then_inc(probs_turned, 1)
                elif kind == "pv":
                    if step[1] < 2 * NB - 1:
                        pv(step[1])
                elif kind == "pool":
                    n, g = MAIN_AT[step], step[2]
                    wait_main_bank(n)
                    pe.wait_ge(pool_in, POOLS.index(step[1:]) + 1)
                    c = slice(g * P, (g + 1) * P)
                    three(main_bank[n % 2][:, :], pw_hi[:, c], pw_lo[:, c], d_hi[:, :], d_lo[:, :],
                          True, True).then_inc(main_made, 1)
                elif kind == "wout":
                    n, m, a = MAIN_AT[step], MIXU_AT[step], step[1]
                    wait_main_bank(n)
                    pe.wait_ge(unit_split, S_MIX + m + 1)
                    pe.wait_ge(pool_split, NG * (a + 1))
                    if a == 1 and step[2] == 0:
                        def ahead():
                            pv(2 * NB - 1)
                            pe.wait_ge(attn_split, 2 * NB)

                        order = [*range(HPK, KT), 0, *range(1, HPK)]
                        eight(main_bank[n % 2], m % MIX_SLOTS, a, order=order, ahead=ahead).then_inc(main_made, 1)
                    else:
                        pe.wait_ge(attn_split, NB * (a + 1))
                        eight(main_bank[n % 2], m % MIX_SLOTS, a).then_inc(main_made, 1)

            pe.wait_ge(res_added, RES_FFN + RES_MIX)
            ffn(1, S_FFN2)

            pe.wait_ge(product_made, 2 * GU)
            for a in (0, 1):
                for d in range(KT):
                    n, m = MAIN_AT[("gate", a, d)], a * KT + d
                    if m >= 2:
                        wait_main_bank(n)
                    pe.wait_ge(unit_split, S_GATE + m + 1)
                    eight(main_bank[n % 2], m % MIX_SLOTS, a, 6 + a if d == 0 else None).then_inc(main_made, 1)
                    if m == 0:
                        norm_sum(7)

        @block.scalar
        def _(act):
            def square(nrm, k, src):
                dst = acc[nrm % 2] if k == 0 else sq[k % 2]
                if k == 0:
                    if nrm >= 2:
                        act.wait_ge(sum_made, nrm - 1)
                elif k <= 2:
                    if nrm >= 1:
                        act.wait_ge(squares_added, acc_count(nrm, 0))
                else:
                    act.wait_ge(squares_added, acc_count(nrm, k - 2))
                act.activation(dst[:, :], src, ACT.Square).then_inc(square_made, 1)

            def std(nrm):
                act.wait_ge(sum_made, nrm + 1)
                if nrm >= 2:
                    act.wait_ge(h_normed, h_count(nrm - 2, KT - 1))
                act.activation(rstd[nrm % 2][:, :], sum_bank[:, :], ACT.Sqrt, bias=col(C_EPS),
                               scale=1.0 / D_MODEL).then_inc(std_made, 1)

            def round_h(nrm, k):
                act.wait_ge(h_normed, h_count(nrm, k))
                act.activation(h_hi[:, k, tok(nrm % 2)], hn[k % 2][:, :], ACT.Copy).then_inc(h_rounded, 1)

            def ffn(ph):
                def silu_tile(g, i):
                    act.wait_ge(gate_made, g * (2 * GF) + (ph * GU + i + 1))
                    act.activation(silu[i % 2][:, :], gate_bank[i % 2][:, :], ACT.Silu).then_inc(silu_made, 1)

                def round_tile(g, i):
                    act.wait_ge(product_made, g * (2 * GF) + (ph * GU + i + 1))
                    act.activation(act_hi[:, i % GF, tok(i // GF)], prod[i % 2][:, :], ACT.Copy).then_inc(act_rounded, 1)

                with act.Fori(0, GROUPS - 1) as g:
                    for i in range(2 * GF):
                        silu_tile(g, i)
                        round_tile(g, i)
                g = GROUPS - 1
                r0 = ph * (RES_FFN + RES_MIX) + 2 * KT * g
                for i in range(2 * GF - 1):
                    silu_tile(g, i)
                    round_tile(g, i)
                for k in range(KT):
                    act.wait_ge(res_added, r0 + k + 1)
                    square(4 * ph + 2, k, x_sb[:, k, tok(0)])
                silu_tile(g, 2 * GF - 1)
                std(4 * ph + 2)
                round_tile(g, 2 * GF - 1)
                for k in range(KT):
                    round_h(4 * ph + 2, k)
                    act.wait_ge(res_added, r0 + KT + k + 1)
                    square(4 * ph + 3, k, x_sb[:, k, tok(1)])

            act.dma_start(const_sb[:, :], const).then_inc(const_in, 16)
            act.dma_start(small_sb[:, :], small).then_inc(small_in, 16)
            act.dma_start(oh_sb[:, :], onehot).then_inc(oh_in, 16)
            act.dma_start(rel_sb[0:N_BUCKETS, :], rel).then_inc(rel_in, 16)
            for i in range(4):
                a, k = i // 2, (i % 2) * (KT // 2)
                act.dma_start(x_sb[:, k:k + KT // 2, tok(a)],
                              xT[k * P:(k + KT // 2) * P, tok(a)].rearrange("(k p) t -> p k t", p=P)).then_inc(x_in[i], 16)

            for h in range(N_Q_HEADS):
                act.wait_ge(band_made, h + 1)
                if h >= 4:
                    act.wait_ge(band_out[h % 4], 16)
                act.activation(gband[h % 4][:, :], band_bank[h % 4][:, 0:SKEW], ACT.Copy).then_inc(band_copied, 1)

            def e_tile(n):
                a, d = n // KT, n % KT
                act.wait_ge(main_made, n + 1)
                if n >= 4:
                    act.wait_ge(e_out[n % 4], 16 * (n // 4))
                act.activation(et[n % 4][:, :], main_bank[n % 2][:, :], ACT.Copy).then_inc(e_copied, 1)
                if d > 2:
                    act.wait_ge(e_added, (KT - 1) * a + d - 2)
                elif d and a:
                    act.wait_ge(e_added, KT - 1)
                dst = eacc[a] if d == 0 else esq[d % 2]
                act.activation(dst[:, :], main_bank[n % 2][:, :], ACT.Square).then_inc(e_square, 1)
                act.wait_ge(e_copied, n + 1)
                act.dma_start(e_dram[a, :, d, :], et[n % 4][:, :]).then_inc(e_out[n % 4], 16)

            act.wait_ge(small_in, 16)
            for k in range(KT):
                e_tile(k)
                act.wait_ge(x_in[k // (KT // 2)], 16)
                square(0, k, x_sb[:, k, tok(0)])
            std(0)
            for k in range(KT):
                e_tile(KT + k)
                round_h(0, k)
                act.wait_ge(x_in[2 + k // (KT // 2)], 16)
                square(1, k, x_sb[:, k, tok(1)])
            std(1)
            for k in range(KT):
                round_h(1, k)
            for a in (0, 1):
                act.wait_ge(e_sum, a + 1)
                act.activation(eacc[a][:, :], sum_bank[:, :], ACT.Sqrt, bias=col(C_EPS), scale=1.0 / D_MODEL).then_inc(e_std, 1)
            for i in range(4):
                act.wait_ge(band_out[i], 32)
            act.wait_ge(e_added, 2 * (KT - 1))
            skewed = bass.AP(tensor=band.tensor, offset=P - 1, ap=[[SKEW - 1, P], [P * SKEW, N_Q_HEADS], [1, 2 * P]])
            act.dma_start(bias[:, :, :], skewed).then_inc(bias_in, 16)
            for a in (0, 1):
                act.wait_ge(e_rstd, a + 1)
                act.dma_start(e_dram[a, :, KT, :], eacc[a][:, :]).then_inc(re_out[a], 16)
            for i in range(4):
                act.wait_ge(e_out[i], 16 * (2 * KT // 4))
            ffn(0)

            for a in (0, 1):
                act.wait_ge(re_out[a], 16)
            for step in PLAN:
                kind = step[0]
                if kind == "win":
                    n, a, what, i = MAIN_AT[step], *step[1:]
                    ps = main_bank[n % 2][:, :]
                    act.wait_ge(main_made, n + 1)
                    if what == "v":
                        if a:
                            act.wait_ge(v_turned, a)
                        act.activation(vT[:, :], ps, ACT.Copy).then_inc(main_copied, 1)
                    elif what == "u":
                        if a:
                            act.wait_ge(pool_in, i + 1)
                        act.activation(ub[:, i, HALO:UB], ps, ACT.Copy).then_inc(main_copied, 1)
                    else:
                        dst = k_sb[:, tok(a)] if what == "k" else q_sb[:, i, tok(a)]
                        j = QKS_AT[(a, what, i)]
                        act.activation(dst, ps, ACT.Copy).then_inc(main_copied, 1)
                        act.wait_ge(main_copied, copied(step))
                        if j >= 2:
                            act.wait_ge(qk_normed, j - 1)
                        act.activation(qb[j % 2][:, :], dst, ACT.Square).then_inc(qk_square, 1)
                elif kind == "qks":
                    i, q = QKS_AT[step[1:]], step[2] == "q"
                    act.wait_ge(qk_sum, i + 1)
                    act.activation(qb[i % 2][:, :], sum_bank[:, :], ACT.Sqrt, bias=col(C_EPSQ if q else C_EPS),
                                   scale=1.0 if q else 1.0 / HEAD_DIM).then_inc(qk_std, 1)
                elif kind == "vt":
                    a = step[1]
                    act.wait_ge(v_turned, a + 1)
                    act.activation(v_sb[:, a * HB:(a + 1) * HB, :], sum_bank[:, :].rearrange("p (b c) -> p b c", b=HB),
                                   ACT.Copy).then_inc(v_copied, 1)
                elif kind == "norm":
                    std(step[1])
                elif kind == "tile":
                    if step[2] < KT:
                        round_h(*step[1:])
                elif kind == "scores":
                    u = step[1]
                    off = P if u < 2 else 0
                    act.wait_ge(max_made, u + 1)
                    act.activation(stats[:, ES, :], stats[:, SM, :], ACT.Exp)
                    for h in range(HPK):
                        last = act.activation(probs[:, h, off:], probs[:, h, off:], ACT.Exp, bias=stats[:, NEGM, h:h + 1],
                                              accum_out=stats[:, DEN, h:h + 1])
                    last.then_inc(exp_made, 1)
                elif kind == "probs":
                    u = step[1]
                    act.wait_ge(probs_turned, u + 1)
                    if u:
                        act.wait_ge(pv_made, u)
                    for kb in ((1,) if u < 2 else (0, 1)):
                        last = act.activation(probsT[:, kb, :], probsT_bank[kb][:, :], ACT.Copy)
                    last.then_inc(probsT_copied, 1)
                elif kind == "pv":
                    u = step[1]
                    b, p0 = u // 2, (u % 2) * HEAD_DIM
                    act.wait_ge(pv_made, u + 1)
                    act.activation(h_hi[p0:p0 + HEAD_DIM, 0:HPK, b * P:(b + 1) * P],
                                   pv_bank[p0:p0 + HEAD_DIM, :].rearrange("p (h q) -> p h q", h=HPK),
                                   ACT.Copy).then_inc(attn_rounded, 1)
                elif kind == "pool":
                    n, a, g = MAIN_AT[step], *step[1:]
                    act.wait_ge(main_made, n + 1)
                    act.activation(h_hi[:, HPK + g, tok(a)], main_bank[n % 2][:, :], ACT.Copy,
                                   scale=col(C_PSCALE + g)).then_inc(pool_rounded, 1)
                elif kind == "wout":
                    a, d = step[1:]
                    act.wait_ge(res_added, RES_FFN + a * KT + d + 1)
                    square(4 + a, d, x_sb[:, d, tok(a)])
            ffn(1)

            for a in (0, 1):
                for d in range(KT):
                    n, m = MAIN_AT[("gate", a, d)], a * KT + d
                    act.wait_ge(main_made, n + 1)
                    if m >= 2:
                        act.wait_ge(y_made, m - 1)
                    act.activation(silu[m % 2][:, :], main_bank[n % 2][:, :], ACT.Sigmoid,
                                   bias=col(C_BGATE + d)).then_inc(sig_made, 1)
                    if m == 0:
                        std(7)
                    for k in range(2 * m, min(2 * m + 2, KT)):
                        round_h(7, k)

        @block.vector
        def _(dve):
            steps = [0]

            def link(ins):
                steps[0] += 1
                ins.then_inc(dve_step, 1)
                dve.wait_ge(dve_step, steps[0])

            def accumulate(nrm, k):
                dve.wait_ge(square_made, sq_count(nrm, k))
                if k >= 2:
                    dve.wait_ge(squares_added, acc_count(nrm, k - 1))
                a = acc[nrm % 2][:, :]
                dve.tensor_tensor(a, a, sq[k % 2][:, :], ALU.add).then_inc(squares_added, 1)

            def reciprocal(nrm):
                r = rstd[nrm % 2][:, :]
                dve.wait_ge(std_made, nrm + 1)
                dve.reciprocal(r, r).then_inc(rstd_made, 1)
                dve.wait_ge(rstd_made, nrm + 1)

            def norm_tile(nrm, k):
                if h_count(nrm, k) > 2:
                    dve.wait_ge(h_split, h_count(nrm, k) - 2)
                g = C_GAIN[nrm // 2] + k
                dve.scalar_tensor_tensor(hn[k % 2][:, :], x_sb[:, k, tok(nrm % 2)], col(g), rstd[nrm % 2][:, :],
                                         ALU.mult, ALU.mult).then_inc(h_normed, 1)

            def split_tile(nrm, k):
                dve.wait_ge(h_rounded, h_count(nrm, k))
                a = tok(nrm % 2)
                dve.tensor_tensor(h_lo[:, k, a], hn[k % 2][:, :], plain(h_hi[:, k, a]), ALU.subtract).then_inc(h_split, 1)

            def tile(nrm, k):
                if k < KT:
                    norm_tile(nrm, k)
                if k:
                    split_tile(nrm, k - 1)

            def ffn(ph):
                def product(g, i):
                    t = ph * GU + i + 1
                    dve.wait_ge(up_made, g * (2 * GF) + t)
                    dve.wait_ge(silu_made, g * (2 * GF) + t)
                    if i >= 2:
                        dve.wait_ge(act_split, g * (2 * GF) + t - 2)
                    dve.tensor_tensor(prod[i % 2][:, :], silu[i % 2][:, :], up_bank[i % 2][:, :], ALU.mult).then_inc(product_made, 1)
                    dve.wait_ge(act_rounded, g * (2 * GF) + t)
                    f, a = i % GF, tok(i // GF)
                    dve.tensor_tensor(act_lo[:, f, a], prod[i % 2][:, :], plain(act_hi[:, f, a]), ALU.subtract).then_inc(act_split, 1)

                def residual(g, r):
                    dve.wait_ge(down_made, g * (2 * KT) + (ph * RES_FFN + r + 1))
                    x = x_sb[:, r % KT, tok(r // KT)]
                    dve.scalar_tensor_tensor(x, down_bank[r % 3][:, :], MACARON_WEIGHT, x, ALU.mult, ALU.add).then_inc(res_added, 1)

                with dve.Fori(0, GROUPS - 1) as g:
                    for i in range(2 * GF):
                        product(g, i)
                    for r in range(2 * KT):
                        residual(g, r)
                g, na = GROUPS - 1, 4 * ph + 2
                for i in range(2 * GF - 1):
                    product(g, i)
                for k in range(KT):
                    residual(g, k)
                    if k >= 2:
                        accumulate(na, k - 1)
                accumulate(na, KT - 1)
                reciprocal(na)
                norm_tile(na, 0)
                product(g, 2 * GF - 1)
                for k in range(KT):
                    residual(g, KT + k)
                    if k + 1 < KT:
                        norm_tile(na, k + 1)
                    split_tile(na, k)

            dve.memset(rel_sb[N_BUCKETS:N_BUCKETS + 1, :], 1.0).then_inc(rel_one, 1)
            dve.wait_ge(rel_one, 1)
            dve.wait_ge(rel_in, 16)
            dve.wait_ge(const_in, 16)
            for h in range(N_Q_HEADS):
                dve.tensor_scalar(relb[:, h, :], const_sb[0:N_BUCKETS + 1, K_ONES:K_ONES + P], rel_sb[:, h:h + 1], None,
                                  ALU.mult).then_inc(rel_spread, 1)
            dve.wait_ge(p_in, 16)
            for k in range(PT_TILES):
                dve.tensor_copy(act_hi[:, k, :], p_raw[:, k, :]).then_inc(p_rounded, 1)
            for k in range(PT_TILES):
                dve.wait_ge(p_rounded, k + 1)
                dve.tensor_tensor(act_lo[:, k, :], p_raw[:, k, :], plain(act_hi[:, k, :]), ALU.subtract).then_inc(p_split, 1)

            def e_accumulate(a, k):
                dve.wait_ge(e_square, a * KT + k + 1)
                if k >= 2:
                    dve.wait_ge(e_added, (KT - 1) * a + k - 1)
                dve.tensor_tensor(eacc[a][:, :], eacc[a][:, :], esq[k % 2][:, :], ALU.add).then_inc(e_added, 1)

            dve.wait_ge(small_in, 16)
            for k in range(1, KT):
                e_accumulate(0, k)
                accumulate(0, k)
            reciprocal(0)
            for k in range(KT + 1):
                tile(0, k)
                if 1 < k:
                    e_accumulate(1, k - 1)
                    accumulate(1, k - 1)
            reciprocal(1)
            for k in range(KT + 1):
                tile(1, k)
            for a in (0, 1):
                dve.wait_ge(e_std, a + 1)
                dve.reciprocal(eacc[a][:, :], eacc[a][:, :]).then_inc(e_rstd, 1)
            ffn(0)

            link(dve.memset(ub[:, :, 0:HALO], 0.0))
            dve.wait_ge(bias_in, 16)
            for step in PLAN:
                kind = step[0]
                if kind == "norm":
                    nrm = step[1]
                    if nrm > 3:
                        accumulate(nrm, KT - 1)
                    reciprocal(nrm)
                elif kind == "tile":
                    tile(*step[1:])
                elif kind == "qks":
                    a, what, i = step[1:]
                    j = QKS_AT[step[1:]]
                    dve.wait_ge(qk_std, j + 1)
                    link(dve.reciprocal(qb[j % 2][:, :], qb[j % 2][:, :]))
                    t = k_sb[:, tok(a)] if what == "k" else q_sb[:, i, tok(a)]
                    dve.scalar_tensor_tensor(t, t, col(C_KN if what == "k" else C_QN), qb[j % 2][:, :],
                                             ALU.mult, ALU.mult).then_inc(qk_normed, 1)
                elif kind == "scores":
                    u = step[1]
                    kv, off = u % 2, (P if u < 2 else 0)
                    dve.wait_ge(scores_made, u + 1)
                    for h in range(HPK):
                        c = (h % 2) * 2 * P
                        hh = kv * HPK + h
                        dve.tensor_tensor_reduce(probs[:, h, off:], score_bank[h // 2][:, c + off:c + 2 * P],
                                                 bias[:, hh, off:], 1.0, col(C_SINK + hh), ALU.add, ALU.max,
                                                 stats[:, MX, h:h + 1]).then_inc(scores_biased, 1)
                    dve.wait_ge(scores_biased, HPK * (u + 1))
                    link(dve.tensor_scalar(stats[:, NEGM, :], stats[:, MX, :], -1.0, None, ALU.mult))
                    c = C_SINK + kv * HPK
                    dve.tensor_tensor(stats[:, SM, :], stats[:, NEGM, :], small_sb[:, c:c + HPK], ALU.add).then_inc(max_made, 1)
                    dve.wait_ge(exp_made, u + 1)
                    link(dve.tensor_tensor(stats[:, RCP, :], stats[:, DEN, :], stats[:, ES, :], ALU.add))
                    link(dve.reciprocal(stats[:, RCP, :], stats[:, RCP, :]))
                    for h in range(HPK):
                        dve.tensor_scalar(probs[:, h, off:], probs[:, h, off:], stats[:, RCP, h:h + 1], None,
                                          ALU.mult).then_inc(probs_normed, 1)
                elif kind == "pv":
                    u = step[1]
                    b, p0 = u // 2, (u % 2) * HEAD_DIM
                    at = (slice(p0, p0 + HEAD_DIM), slice(0, HPK), slice(b * P, (b + 1) * P))
                    dve.wait_ge(attn_rounded, u + 1)
                    dve.tensor_tensor(h_lo[at], pv_bank[p0:p0 + HEAD_DIM, :].rearrange("p (h q) -> p h q", h=HPK),
                                      plain(h_hi[at]), ALU.subtract).then_inc(attn_split, 1)
                elif kind == "prep":
                    a, g = step[1:]
                    u, w, i = ub[:, g, :], POOL_WINDOWS[g], POOLS.index((a, g))
                    if i:
                        dve.wait_ge(pool_in, i)
                    dve.wait_ge(main_copied, copied(("win", a, "u", g)))
                    s, reach = u, 1
                    bufs = [win_a, win_b]
                    while reach < w:
                        dst = bufs[0][:, :]
                        bufs.reverse()
                        lo = 2 * reach - 1
                        link(dve.tensor_tensor(dst[:, lo:UB], s[:, lo:UB], s[:, lo - reach:UB - reach], ALU.add))
                        s, reach = dst, 2 * reach
                    body = slice(2 * HALO, UB) if a == 0 else slice(HALO, UB)
                    ins = dve.scalar_tensor_tensor(s[:, body], s[:, body], 1.0 / w, u[:, body], ALU.mult, ALU.subtract)
                    if a == 0:
                        first = slice(HALO, 2 * HALO)
                        link(ins)
                        c = K_RC + g * HALO
                        link(dve.tensor_tensor(s[:, first], s[:, first], const_sb[:, c:c + HALO], ALU.mult))
                        ins = dve.tensor_tensor(s[:, first], s[:, first], u[:, first], ALU.subtract)
                    link(ins)
                    if i:
                        dve.wait_ge(main_made, MAIN_AT[("pool", *POOLS[i - 1])] + 1)
                    link(dve.tensor_copy(d_hi[:, :], s[:, HALO:UB]))
                    link(dve.tensor_tensor(d_lo[:, :], s[:, HALO:UB], plain(d_hi[:, :]), ALU.subtract))
                    dve.tensor_copy(u[:, 0:HALO], u[:, HALF:UB]).then_inc(pool_in, 1)
                elif kind == "pool":
                    n, a, g = MAIN_AT[step], *step[1:]
                    dve.wait_ge(pool_rounded, POOLS.index((a, g)) + 1)
                    dve.scalar_tensor_tensor(h_lo[:, HPK + g, tok(a)], main_bank[n % 2][:, :], col(C_PSCALE + g),
                                             plain(h_hi[:, HPK + g, tok(a)]), ALU.mult, ALU.subtract).then_inc(pool_split, 1)
                elif kind == "wout":
                    n, a, d = MAIN_AT[step], *step[1:]
                    if d == 0:
                        dve.wait_ge(res_added, RES_FFN + a * KT)
                    dve.wait_ge(main_made, n + 1)
                    x = x_sb[:, d, tok(a)]
                    dve.tensor_tensor(x, x, main_bank[n % 2][:, :], ALU.add).then_inc(res_added, 1)
                    if d >= 2:
                        accumulate(4 + a, d - 1)
            ffn(1)

            def finish(m):
                a, d = m // KT, m % KT
                e = e_sb[a][:, d, :]
                x = x_sb[:, d, tok(a)]
                dve.wait_ge(e_in[a], 32)
                link(dve.scalar_tensor_tensor(e, e, col(C_G["post"] + d), re_sb[:, a, :], ALU.mult, ALU.mult))
                dve.wait_ge(sig_made, m + 1)
                link(dve.tensor_tensor(e, e, silu[m % 2][:, :], ALU.mult))
                dve.tensor_tensor(x, x, e, ALU.add).then_inc(y_made, 1)

            for m in range(2 * KT):
                finish(m)
                if m == 0:
                    reciprocal(7)
                for k in range(2 * m, min(2 * m + 2, KT + 1)):
                    tile(7, k)


def build(nc, xT, pT, units, poolw, small, const, onehot, rel, out):
    band = nc.dram_tensor("band", (N_Q_HEADS, P, SKEW), F32, kind="Internal").ap()
    e_dram = nc.dram_tensor("e_dram", (2, P, KT + 1, HALF), F32, kind="Internal").ap()
    program(nc, xT, pT, units, poolw, small, const, onehot, rel, band, e_dram, out)


def constants():
    c = np.zeros((P, N_CONST), np.float32)
    c[:, K_ID:K_ID + P] = np.eye(P)
    c[:, K_ONES:K_ONES + P] = 1.0
    c[:, K_BLK:K_BLK + P] = np.kron(np.eye(P // HEAD_DIM), np.ones((HEAD_DIM, HEAD_DIM)))
    for g, w in enumerate(POOL_WINDOWS):
        c[:, K_RC + g * HALO:K_RC + (g + 1) * HALO] = 1.0 / np.minimum(np.arange(HALO) + 1, w)
    return c


def onehots():
    oh = np.zeros((N_BUCKETS + 1, SKEW), np.float32)
    half = N_BUCKETS // 2
    for i in range(SKEW):
        n = 2 * P - 1 - i
        if 0 <= n < WINDOW:
            b = n if n < half else min(N_BUCKETS - 1, half + int(
                math.log(n / half) / math.log(MAX_DISTANCE / half) * (N_BUCKETS - half) + 1e-9))
            oh[b, i] = 1.0
        else:
            oh[N_BUCKETS, i] = NEG_INF
    return oh


def pack_ffn(w_gu, w_down):
    gu = w_gu.reshape(KT, P, 2, GROUPS, GF, P).transpose(3, 4, 2, 1, 0, 5).reshape(GROUPS, 2 * GF, P, UNIT)
    dn = w_down.reshape(GROUPS, GF, P, D_MODEL)
    return np.concatenate([gu, dn], axis=1).reshape(FFN_UNITS, P, UNIT)


def pack_square(w):
    n = w.shape[1] // P
    return w.reshape(KT, P, n, P).transpose(2, 1, 0, 3).reshape(n, P, UNIT)


def kernel(x, p, ffn1_norm, ffn1_w_gu, ffn1_w_down, mix_norm, w_in, q_norm, k_norm,
           rel_bias, sinks, pool_w, pool_scale, w_out, ffn2_norm, ffn2_w_gu, ffn2_w_down,
           ple_norm, ple_w_gate, ple_b_gate, ple_w_proj, ple_post_norm):
    import concourse.bacc as bacc
    from concourse.bass_utils import run_bass_kernel_spmd

    f = np.ascontiguousarray
    heads = np.arange(ATTN_WIDTH).reshape(N_KV_HEADS, HPK, HEAD_DIM).transpose(1, 0, 2).reshape(-1)
    w_in = np.asarray(w_in)[0]
    w_in = np.concatenate([w_in[:, heads], w_in[:, ATTN_WIDTH:]], axis=1)
    w_out = np.asarray(w_out)[0]
    w_out = np.concatenate([w_out[heads], w_out[ATTN_WIDTH:]], axis=0)
    proj = np.asarray(ple_w_proj)[0].reshape(PT_TILES, P, 2, KT // 2, P).transpose(2, 1, 3, 0, 4).reshape(2, P, UNIT)
    units = np.concatenate([
        proj, pack_ffn(np.asarray(ffn1_w_gu)[0], np.asarray(ffn1_w_down)[0]), pack_square(w_in), pack_square(w_out),
        pack_ffn(np.asarray(ffn2_w_gu)[0], np.asarray(ffn2_w_down)[0]), pack_square(np.asarray(ple_w_gate)[0])])

    def by_partition(v):
        return np.asarray(v)[0].reshape(-1, P).T

    def twice(v):
        return np.tile(np.asarray(v)[0], P // HEAD_DIM)[:, None]

    eps = np.zeros((P, 2), np.float32)
    eps[:, 0], eps[:, 1] = EPS, EPS * HEAD_DIM
    small = np.concatenate([
        by_partition(ffn1_norm), by_partition(mix_norm), by_partition(ffn2_norm), by_partition(ple_norm),
        by_partition(ple_post_norm), by_partition(ple_b_gate), by_partition(pool_scale), twice(q_norm), twice(k_norm),
        np.broadcast_to(np.asarray(sinks), (P, N_Q_HEADS)), eps], axis=1)
    arrays = {
        "xT": f(np.asarray(x)[0].T), "pT": f(np.asarray(p)[0, 0].T), "units": f(units),
        "poolw": f(np.asarray(pool_w)[0].transpose(1, 0, 2).reshape(P, NG * P)), "small": f(small),
        "const": constants(), "onehot": onehots(), "rel": f(np.asarray(rel_bias)),
    }
    nc = bacc.Bacc("TRN2", target_bir_lowering=False, num_devices=1, dynamic_dma_scratch_size=1024)
    args = [nc.dram_tensor(f"in_{k}", v.shape, mybir.dt.from_np(v.dtype), kind="ExternalInput").ap()
            for k, v in arrays.items()]
    out = nc.dram_tensor("outT", (D_MODEL, SEQ), F32, kind="ExternalOutput").ap()
    build(nc, *args, out)
    r = run_bass_kernel_spmd(nc, [{f"in_{k}": v for k, v in arrays.items()}], core_ids=[0])
    return f(r.results[0]["outT"].T)[None]
```

```python
import math
from contextlib import ExitStack

import numpy as np

import concourse.bass as bass
from concourse import mybir

F32 = mybir.dt.float32
F32R = mybir.dt.float32r
ACT = mybir.ActivationFunctionType
ALU = mybir.AluOpType

P = 128
D_MODEL = 1024
SEQ = 1024
N_Q_HEADS = 8
N_KV_HEADS = 2
HEAD_DIM = 64
ATTN_WIDTH = N_Q_HEADS * HEAD_DIM
N_BUCKETS = 32
MAX_DISTANCE = 128
WINDOW = 128
POOL_WINDOWS = (2, 4, 8, 16)
D_FF = 2816
PLE_DIM = 256
MACARON_WEIGHT = 0.5
EPS = 1e-6
NEG_INF = -1e30

KT = D_MODEL // P
PT_TILES = PLE_DIM // P
HALF = SEQ // 2
NB = SEQ // P
HB = NB // 2
HPK = N_Q_HEADS // N_KV_HEADS
NG = len(POOL_WINDOWS)
HALO = max(POOL_WINDOWS)
FT = D_FF // P
GF = 2
GROUPS = FT // GF
UNIT = KT * P
SKEW = 3 * P

C_G = {"ffn1": 0, "mix": 8, "ffn2": 16, "ple": 24, "post": 32}
C_BGATE, C_PSCALE, C_QN, C_KN, C_SINK, C_EPS, C_EPSQ = 40, 48, 52, 53, 54, 62, 63
N_SMALL = 64
C_GAIN = [C_G["ffn1"], C_G["mix"], C_G["ffn2"], C_G["ple"]]
K_ID, K_ONES, K_BLK, K_RC = 0, P, 2 * P, 3 * P
N_CONST = K_RC + NG * HALO

W_PROJ, W_FFN1 = 0, 2
FFN_UNITS = 3 * FT
W_IN = W_FFN1 + FFN_UNITS
N_IN = 10
W_OUT = W_IN + N_IN
W_FFN2 = W_OUT + KT
W_GATE = W_FFN2 + FFN_UNITS
NRAW = 2
N_MIXU = 2 * N_IN + 2 * KT
S_PROJ, S_POOLW = 0, 2
S_FFN1 = S_POOLW + 1
S_MIX = S_FFN1 + FFN_UNITS
S_FFN2 = S_MIX + N_MIXU
S_GATE = S_FFN2 + FFN_UNITS
EARLY = 3
LAG = 5
MIX_SLOTS = 2 * GF
DN_SLOT = 2 * GF

GU = 2 * FT
RES_FFN = 2 * KT * GROUPS
RES_MIX = 2 * KT

COL_Q, COL_K, COL_V, COL_U = 0, 4, 5, 6
POOLS = [(a, g) for a in (0, 1) for g in range(NG)]


def mix_plan():
    def win(a, what, i=0):
        return ("win", a, what, i)

    plan = [win(0, "k"), win(0, "v"), ("qks", 0, "k", 0), win(0, "q", 0), ("norm", 3)]

    def pooling(u):
        i = u // 2
        return [("pool", *POOLS[i])] + [("prep", *x) for x in POOLS[i + 1:i + 2]] if u % 2 == 0 else []

    order = [win(0, "q", t) for t in range(1, HPK)] + [win(0, "u", g) for g in range(NG)] + [win(1, "k")]
    tiles = [0, 1, 1, 1, 2, 2, 2, 0]
    for j, step in enumerate(order):
        plan.append(step)
        plan += [("qks", 0, "q", j)] if j < HPK else [("vt", 0)] if j == HPK else []
        plan += [("tile", 3, k) for k in range(sum(tiles[:j]), sum(tiles[:j + 1])) if k <= KT]
        if step == win(0, "u", 0):
            plan.append(("prep", 0, 0))
    fill = [win(1, "v"), win(1, "u", 0), win(1, "q", 0), win(1, "u", 1), win(1, "q", 1), win(1, "q", 2),
            win(1, "q", 3), win(1, "u", 2)]
    ready = {0: [("qks", 1, "k", 0)], 1: [("vt", 1)], 3: [("qks", 1, "q", 0)], 5: [("qks", 1, "q", 1)],
             6: [("qks", 1, "q", 2)], 7: [("qks", 1, "q", 3)]}
    for u in range(NB):
        plan.append(("scores", u))
        plan += ready.get(u, [])
        plan.append(fill[u])
        plan += pooling(u)
        if u:
            plan.append(("pv", u - 1))
        plan.append(("probs", u))
    plan += [win(1, "u", NG - 1), ("pv", NB - 1)]
    for u in range(NB, 2 * NB):
        g = u - NB
        plan += [("scores", u), ("wout", 0, g)]
        plan += pooling(u)
        if u > NB:
            plan.append(("pv", u - 1))
        plan.append(("probs", u))
    plan += [("wouts",), ("pv", 2 * NB - 1), ("norm", 4)]
    for d in range(KT):
        plan.append(("wout", 1, d))
        if d:
            plan += [("tile", 4, k) for k in range(2 * d - 2, 2 * d) if k <= KT]
    return plan


PLAN = mix_plan()


def dram_unit(what, i):
    return W_IN + {"q": COL_Q, "k": COL_K, "v": COL_V, "u": COL_U}[what] + i


MAIN = [("proj", a, d) for a in (0, 1) for d in range(KT)]
MAIN += [s for s in PLAN if s[0] in ("win", "pool", "wout")]
MAIN += [("gate", a, d) for a in (0, 1) for d in range(KT)]
MAIN_AT = {s: n for n, s in enumerate(MAIN)}
MIXU = [s for s in PLAN if s[0] in ("win", "wout")]
MIXU_AT = {s: m for m, s in enumerate(MIXU)}
assert len(MIXU) == N_MIXU and N_MIXU % MIX_SLOTS == 0
N_GATE0 = MAIN_AT[("gate", 0, 0)]


def unit_of(step):
    return dram_unit(step[2], step[3]) if step[0] == "win" else W_OUT + step[2]


def freed_table():
    kinds = {"esq": 0, "act": 0, "lo": 0, "res": RES_FFN, "sig": 0}
    out = []
    for s in MAIN:
        if s[0] == "proj":
            k = "esq"
        elif s[0] == "win":
            k = "act"
        elif s[0] == "pool":
            k = "lo"
        elif s[0] == "wout":
            k = "res"
        else:
            k = "sig"
        kinds[k] += 1
        out.append((k, kinds[k]))
    return out


FREED = freed_table()

BANK7 = [("norm", 0), ("norm", 1), ("e", 0), ("e", 1), ("norm", 2)]
BANK7 += [s for s in PLAN if s[0] in ("norm", "qks", "vt")] + [("norm", 5), ("norm", 6), ("norm", 7)]
BANK7_AT = {s: i for i, s in enumerate(BANK7)}
QKS = [s for s in PLAN if s[0] == "qks"]
QKS_AT = {s[1:]: i for i, s in enumerate(QKS)}


def program(nc, xT, pT, units, poolw, small, const, onehot, rel, band, e_dram, out):
    with ExitStack() as ctx:
        cursor = [-(-nc.sbuf_base // 64) * 64]

        def place(name, shape, dt=F32, at=None):
            size = 4 * int(np.prod(shape[1:]))
            where = cursor[0] if at is None else at
            if at is None:
                cursor[0] += -(-size // 32) * 32
            return nc.alloc_sbuf_tensor_at(name, list(shape), dt, offset=where), where

        x_sb, _ = place("x_sb", (P, KT, SEQ))
        h_hi, h_at = place("h_hi", (P, KT, SEQ), F32R)
        h_lo, _ = place("h_lo", (P, KT, SEQ), F32R)
        w_hi, w_lo = [], []
        for s in range(3 * GF):
            if s == DN_SLOT:
                dn_at = cursor[0]
            w_hi.append(place(f"w_hi{s}", (P, UNIT), F32R)[0])
            w_lo.append(place(f"w_lo{s}", (P, UNIT), F32R)[0])
        dn_end = cursor[0]
        raw = [place(f"raw{i}", (P, UNIT))[0] for i in range(NRAW)]
        act_hi, act_at = place("act_hi", (P, GF, SEQ), F32R)
        act_lo, _ = place("act_lo", (P, GF, SEQ), F32R)
        work_at = cursor[0]
        silu = [place(f"silu{i}", (P, HALF))[0] for i in range(2)]
        prod = [place(f"prod{i}", (P, HALF))[0] for i in range(2)]
        acc, acc_at = zip(*(place(f"acc{a}", (P, HALF)) for a in (0, 1)))
        sq = [place(f"sq{i}", (P, HALF))[0] for i in range(2)]
        rstd, rstd_at = zip(*(place(f"rstd{a}", (P, HALF)) for a in (0, 1)))
        hn, hn_at = zip(*(place(f"hn{i}", (P, HALF)) for i in range(2)))
        bias, bias_at = place("bias", (P, N_Q_HEADS, 2 * P))
        pw_hi, _ = place("pw_hi", (P, NG * P), F32R)
        pw_lo, _ = place("pw_lo", (P, NG * P), F32R)
        small_sb, _ = place("small_sb", (P, N_SMALL))
        const_sb, _ = place("const_sb", (P, N_CONST))
        stats, _ = place("stats", (P, 6, HPK))
        rel_sb, _ = place("rel_sb", (N_BUCKETS + 1, N_Q_HEADS))
        tick, _ = place("tick", (P, 1))
        zero, _ = place("zero", (P, 1))
        k_sb, mix_at = place("k_sb", (P, SEQ))
        v_hi, _ = place("v_hi", (P, NB, P), F32R)
        d_hi, _ = place("d_hi", (P, HALF), F32R)
        d_lo, _ = place("d_lo", (P, HALF), F32R)
        qb = [place(f"qb{i}", (P, HALF))[0] for i in range(2)]
        assert cursor[0] <= nc.sbuf_usable_end, (cursor[0], nc.sbuf_usable_end)
        q_sb, _ = place("q_sb", (P, HPK, SEQ), at=act_at)
        probs, _ = place("probs", (P, HPK, 2 * P), at=work_at)
        probsT_hi, _ = place("probsT_hi", (P, 2, HPK * P), F32R, at=work_at + 8 * HALF)
        probsT_lo = [place(f"probsT_lo{i}", (P, HPK * P), F32R, at=hn_at[i])[0] for i in range(2)]
        v_lo = [place(f"v_lo{a}", (P, HB, P), F32R, at=at)[0] for a, at in enumerate((acc_at[1], rstd_at[1]))]
        UB = HALO + HALF
        ub, _ = place("ub", (P, NG, UB), at=dn_at)
        win_a, _ = place("win_a", (P, UB), at=dn_at + 4 * NG * UB)
        win_b, _ = place("win_b", (P, UB), at=dn_at + 4 * (NG + 1) * UB)
        vT, _ = place("vT", (P, HALF), at=dn_at + 4 * (NG + 2) * UB)
        assert dn_at + 4 * (NG + 2) * UB + 4 * HALF <= dn_end
        oh_sb, _ = place("oh_sb", (N_BUCKETS + 1, SKEW), at=mix_at)
        relb, _ = place("relb", (N_BUCKETS + 1, N_Q_HEADS, P), at=mix_at + 4 * SKEW)
        gband = [place(f"gband{h}", (P, SKEW), at=h_at + 4 * (h * SEQ + HALF))[0] for h in range(N_Q_HEADS)]
        eacc_at = mix_at + 4 * (SKEW + N_Q_HEADS * P)
        eacc = [place(f"eacc{a}", (P, HALF), at=eacc_at + 4 * a * HALF)[0] for a in (0, 1)]
        assert eacc_at + 8 * HALF <= cursor[0]
        p_raw, _ = place("p_raw", (P, PT_TILES, SEQ), at=bias_at)
        esq = [place(f"esq{i}", (P, HALF), at=bias_at + 4 * i * HALF)[0] for i in range(4)]
        e_sb = [place("e_a", (P, KT, HALF), at=mix_at)[0], place("e_b", (P, KT, HALF), at=act_at)[0]]
        re_sb, _ = place("re_sb", (P, 2, HALF), at=bias_at)
        et = silu + prod

        ident = const_sb[:, K_ID:K_ID + P]
        ones = const_sb[:, K_ONES:K_ONES + P]
        blockones = const_sb[:, K_BLK:K_BLK + P]
        NEGM, SM, ES, DEN, RCP, MX = range(6)

        def col(c):
            return small_sb[:, c:c + 1]

        def tok(a):
            return slice(a * HALF, (a + 1) * HALF)

        def plain(ap):
            return ap.bitcast(F32)

        bank = [ctx.enter_context(nc.psum_tensor(f"bank{i}", [P, 512], F32)) for i in range(8)]
        main_bank, gate_bank, up_bank, down_bank = bank[0:2], bank[0:2], bank[2:4], bank[4:7]
        last_bank = bank[4:7] + bank[2:4]
        band_bank = bank[2:6]
        score_bank, probsT_bank, pv_bank, sum_bank = bank[2:4], bank[4:6], bank[6], bank[7]

        def sem(name):
            return ctx.enter_context(nc.semaphore(name))

        small_in, const_in, oh_in, rel_in = sem("small_in"), sem("const_in"), sem("oh_in"), sem("rel_in")
        x_in = [sem(f"x_in{i}") for i in range(4)]
        raw_in = [sem(f"raw_in{i}") for i in range(NRAW)]
        unit_hi, unit_split = sem("unit_hi"), sem("unit_split")
        zero_made = sem("zero_made")
        p_in, p_rounded, p_split = [sem(f"p_in{a}") for a in (0, 1)], sem("p_rounded"), sem("p_split")
        e_square, e_sum, e_std, e_rstd = (sem(n) for n in ("e_square", "e_sum", "e_std", "e_rstd"))
        e_added = [sem(f"e_added{a}") for a in (0, 1)]
        rel_one, rel_spread, band_made, band_copied = sem("rel_one"), sem("rel_spread"), sem("band_made"), sem("band_copied")
        band_out = sem("band_out")
        bias_in = sem("bias_in")
        e_copied = sem("e_copied")
        e_out = [sem(f"e_out{i}") for i in range(4)]
        re_out = [sem(f"re_out{a}") for a in (0, 1)]
        e_in = [sem(f"e_in{a}") for a in (0, 1)]
        main_made, main_copied, sig_made = sem("main_made"), sem("main_copied"), sem("sig_made")
        gate_made, up_made, silu_made, product_made = sem("gate_made"), sem("up_made"), sem("silu_made"), sem("product_made")
        act_rounded, act_split = sem("act_rounded"), sem("act_split")
        down_made, res_added = sem("down_made"), sem("res_added")
        square_made, squares_added, sum_made = sem("square_made"), sem("squares_added"), sem("sum_made")
        std_made, rstd_made = sem("std_made"), sem("rstd_made")
        h_normed, h_rounded, h_split = sem("h_normed"), sem("h_rounded"), sem("h_split")
        qk_square, qk_sum, qk_std, qk_normed = sem("qk_square"), sem("qk_sum"), sem("qk_std"), sem("qk_normed")
        v_turned, v_rounded, v_split = sem("v_turned"), sem("v_rounded"), sem("v_split")
        pool_in, pool_rounded, pool_split = sem("pool_in"), sem("pool_rounded"), sem("pool_split")
        scores_made, scores_biased, max_made, exp_made = sem("scores_made"), sem("scores_biased"), sem("max_made"), sem("exp_made")
        probs_normed, probs_turned = sem("probs_normed"), sem("probs_turned")
        probsT_rounded, probsT_split = sem("probsT_rounded"), sem("probsT_split")
        pv_made, attn_rounded, attn_split = sem("pv_made"), sem("attn_rounded"), sem("attn_split")
        dve_step, pool_step = sem("dve_step"), sem("pool_step")
        y_made, y_out = sem("y_made"), sem("y_out")

        freed_sem = {"esq": e_square, "act": main_copied, "lo": pool_split, "res": res_added, "sig": sig_made}
        assert FREED[MAIN_AT[PLAN[0]]][1] == 1

        def copied(step):
            kind, value = FREED[MAIN_AT[step]]
            assert kind == "act"
            return value

        def h_count(nrm, k):
            return KT * nrm + k + 1

        def sq_count(nrm, k):
            return KT * nrm + k + 1

        def acc_count(nrm, k):
            return (KT - 1) * nrm + k

        block = ctx.enter_context(nc.Block())

        def store(sp, n):
            a, d = n // KT, n % KT
            sp.wait_ge(y_made, n + 1)
            sp.dma_start(out[d * P:(d + 1) * P, tok(a)], x_sb[:, d, tok(a)]).then_inc(y_out, 16)

        @block.sync
        def _(sp):
            def load(n, src, size=UNIT):
                if n >= NRAW:
                    sp.wait_ge(unit_split, n - NRAW + 1)
                sp.dma_start(raw[n % NRAW][:, 0:size], src).then_inc(raw_in[n % NRAW], 16)

            def ffn_loads(w0, s0, after):
                per = 3 * GF
                assert per % NRAW == 0
                for j in range(2 * GF):
                    load(s0 + j, units[w0 + j])
                with sp.Fori(0, GROUPS - 1) as g:
                    for j in range(per):
                        n = s0 + 2 * GF + j
                        sp.wait_ge(unit_split, g * per + (n - NRAW + 1))
                        src = units[bass.ds(g * per + (w0 + 2 * GF + j), 1), :, :].rearrange("a p n -> (a p) n")
                        sp.dma_start(raw[n % NRAW][:, :], src).then_inc(raw_in[n % NRAW], 16)
                for j in range(GF):
                    load(s0 + FFN_UNITS - GF + j, units[w0 + FFN_UNITS - GF + j])
                for j in range(2 * GF):
                    load(s0 + FFN_UNITS + j, units[after[j]])

            sp.dma_start(rel_sb[0:N_BUCKETS, :], rel).then_inc(rel_in, 16)
            sp.dma_start(oh_sb[:, :], onehot).then_inc(oh_in, 16)
            for a in (0, 1):
                sp.dma_start(p_raw[:, :, tok(a)], pT[:, tok(a)].rearrange("(k p) t -> p k t", p=P)).then_inc(p_in[a], 16)
                load(S_PROJ + a, units[W_PROJ + a])
            for h in range(N_Q_HEADS):
                sp.wait_ge(band_copied, h + 1)
                sp.dma_start(band[h], gband[h][:, :]).then_inc(band_out, 16)
            load(S_POOLW, poolw, NG * P)
            ffn_loads(W_FFN1, S_FFN1, [unit_of(s) for s in MIXU[:MIX_SLOTS]])
            for m in range(MIX_SLOTS, N_MIXU):
                load(S_MIX + m, units[unit_of(MIXU[m])])
            for i in range(4):
                sp.wait_ge(e_out[i], 16 * (2 * KT // 4))
            for a in (0, 1):
                sp.wait_ge(re_out[a], 16)
            sp.wait_ge(pv_made, 2 * NB)
            sp.wait_ge(pool_split, 2 * NG)
            sp.wait_ge(qk_normed, len(QKS))
            sp.wait_ge(scores_biased, HPK * 2 * NB)
            sp.dma_start(e_sb[0][:, :, :], e_dram[0, :, 0:KT, :]).then_inc(e_in[0], 16)
            for a in (0, 1):
                sp.dma_start(re_sb[:, a, :], e_dram[a, :, KT, :]).then_inc(e_in[a], 16)
            ffn_loads(W_FFN2, S_FFN2, [W_GATE + j for j in range(MIX_SLOTS)])
            sp.wait_ge(down_made, 2 * RES_FFN)
            sp.dma_start(e_sb[1][:, :, :], e_dram[1, :, 0:KT, :]).then_inc(e_in[1], 16)
            for m in range(MIX_SLOTS, 2 * KT):
                load(S_GATE + m, units[W_GATE + m % KT])
                if m >= MIX_SLOTS + 4:
                    store(sp, m - MIX_SLOTS - 4)
            for n in range(2 * KT - MIX_SLOTS - 4, 2 * KT):
                store(sp, n)
            sp.wait_ge(y_out, 16 * 2 * KT)

        @block.gpsimd
        def _(pool):
            def split(raw_tile, hi, lo, rounded):
                pool.tensor_scalar(hi, raw_tile, 1.0, 1.0, ALU.mult, ALU.mult).then_inc(unit_hi, 1)
                pool.wait_ge(unit_hi, rounded)
                pool.tensor_tensor(lo, raw_tile, plain(hi), ALU.subtract).then_inc(unit_split, 1)

            def unit(n, hi, lo, size=UNIT):
                pool.wait_ge(raw_in[n % NRAW], 16 * (n // NRAW + 1))
                split(raw[n % NRAW][:, 0:size], hi, lo, n + 1)

            def slot_unit(n, s):
                unit(n, w_hi[s][:, :], w_lo[s][:, :])

            steps = [0]

            def link(ins):
                steps[0] += 1
                ins.then_inc(pool_step, 1)
                pool.wait_ge(pool_step, steps[0])

            def pool_input(a, g):
                u, w, i = ub[:, g, :], POOL_WINDOWS[g], POOLS.index((a, g))
                if i:
                    pool.wait_ge(pool_in, i)
                pool.wait_ge(main_copied, copied(("win", a, "u", g)))
                s, t, reach = u, win_a[:, :], 1
                while reach < w:
                    lo = 2 * reach - 1
                    link(pool.tensor_tensor(t[:, lo:UB], s[:, lo:UB], s[:, lo - reach:UB - reach], ALU.add))
                    s, t, reach = t, (win_b if reach == 1 else s)[:, :], 2 * reach
                body = slice(HALO, UB)
                if a == 0:
                    first, c = slice(HALO, 2 * HALO), K_RC + g * HALO
                    link(pool.tensor_tensor(s[:, first], s[:, first], const_sb[:, c:c + HALO], ALU.mult))
                    body = slice(2 * HALO, UB)
                link(pool.tensor_scalar(s[:, body], s[:, body], 1.0 / w, 1.0, ALU.mult, ALU.mult))
                link(pool.tensor_tensor(s[:, HALO:UB], s[:, HALO:UB], u[:, HALO:UB], ALU.subtract))
                if i:
                    pool.wait_ge(main_made, MAIN_AT[("pool", *POOLS[i - 1])] + 1)
                link(pool.tensor_scalar(d_hi[:, :], s[:, HALO:UB], 1.0, 1.0, ALU.mult, ALU.mult))
                link(pool.tensor_tensor(d_lo[:, :], s[:, HALO:UB], plain(d_hi[:, :]), ALU.subtract))
                pool.tensor_scalar(u[:, 0:HALO], u[:, HALF:UB], 1.0, 1.0, ALU.mult, ALU.mult).then_inc(pool_in, 1)

            def ffn_units(ph, s0):
                per = 3 * GF
                with pool.Fori(0, GROUPS - 1) as g:
                    for j in range(per):
                        n = s0 + 2 * GF + j
                        if j < GF:
                            s, used, count = DN_SLOT + j, gate_made, g * (2 * GF) + (ph * GU + 1)
                        else:
                            s = j - GF
                            used, count = up_made, g * (2 * GF) + (ph * GU + GF + s // 2 + 1)
                        pool.wait_ge(used, count)
                        pool.wait_ge(raw_in[n % NRAW], g * (16 * per // NRAW) + 16 * (n // NRAW + 1))
                        pool.tensor_tensor(tick[:, :], zero[:, :], zero[:, :], ALU.add)
                        split(raw[n % NRAW][:, :], w_hi[s][:, :], w_lo[s][:, :], g * per + (n + 1))
                pool.wait_ge(gate_made, (ph + 1) * GU - 2 * GF + 1)
                for j in range(GF):
                    slot_unit(s0 + FFN_UNITS - GF + j, DN_SLOT + j)
                for s in range(MIX_SLOTS):
                    if s == 3:
                        a = acc[1][:, :]
                        for k in range(1, KT):
                            pool.wait_ge(square_made, sq_count(4 * ph + 3, k))
                            if k >= 2:
                                pool.wait_ge(squares_added, acc_count(4 * ph + 3, k - 1))
                            pool.tensor_tensor(a, a, sq[k % 2][:, :], ALU.add).then_inc(squares_added, 1)
                    pool.wait_ge(up_made, (ph + 1) * GU - GF + s // 2 + 1)
                    slot_unit(s0 + FFN_UNITS + s, s)

            pool.memset(zero[:, :], 0.0).then_inc(zero_made, 1)
            pool.wait_ge(zero_made, 1)
            for j in range(2):
                slot_unit(S_PROJ + j, DN_SLOT + j)
            unit(S_POOLW, pw_hi[:, :], pw_lo[:, :], NG * P)
            for s in (0, 1):
                slot_unit(S_FFN1 + s, s)
            for k in range(1, KT):
                pool.wait_ge(e_square, KT + k + 1)
                if k >= 2:
                    pool.wait_ge(e_added[1], k - 1)
                pool.tensor_tensor(eacc[1][:, :], eacc[1][:, :], esq[k % 4][:, :], ALU.add).then_inc(e_added[1], 1)
            for s in range(2, 2 * GF):
                slot_unit(S_FFN1 + s, s)
            pool.wait_ge(main_made, 2 * KT)
            ffn_units(0, S_FFN1)
            pool.wait_ge(down_made, RES_FFN)
            link(pool.memset(ub[:, :, 0:HALO], 0.0))
            for step in PLAN:
                if step[0] in ("win", "wout"):
                    m = MIXU_AT[step] + MIX_SLOTS
                    pool.wait_ge(main_made, MAIN_AT[step] + 1)
                    slot_unit(S_MIX + m, m % MIX_SLOTS)
                elif step[0] == "prep":
                    pool_input(*step[1:])
            pool.wait_ge(pool_in, 2 * NG)
            pool.wait_ge(v_turned, 2)
            ffn_units(1, S_FFN2)
            for m in range(MIX_SLOTS, 2 * KT):
                pool.wait_ge(main_made, N_GATE0 + m - MIX_SLOTS + 1)
                slot_unit(S_GATE + m, m % MIX_SLOTS)

        @block.tensor
        def _(pe):
            def three(ps, whi, wlo, vhi, vlo, first, last):
                pe.matmul(ps, whi, vhi, start=first, stop=False)
                pe.matmul(ps, whi, vlo, start=False, stop=False)
                return pe.matmul(ps, wlo, vhi, start=False, stop=last)

            def wait_sum_bank(use):
                i = BANK7_AT[use]
                if i:
                    kind, *which = BANK7[i - 1]
                    done = {"e": e_std, "norm": std_made, "qks": qk_std, "vt": v_split}[kind]
                    pe.wait_ge(done, (QKS_AT[tuple(which)] if kind == "qks" else which[0]) + 1)

            def wait_main_bank(n):
                if n >= 2:
                    kind, value = FREED[n - 2]
                    pe.wait_ge(freed_sem[kind], value)

            def norm_sum(nrm):
                pe.wait_ge(squares_added, acc_count(nrm, KT - 1))
                wait_sum_bank(("norm", nrm))
                pe.matmul(sum_bank[:, :], ones, acc[nrm % 2][:, :], start=True, stop=True).then_inc(sum_made, 1)

            def e_sums(a):
                pe.wait_ge(e_added[a], KT - 1)
                wait_sum_bank(("e", a))
                pe.matmul(sum_bank[:, :], ones, eacc[a][:, :], start=True, stop=True).then_inc(e_sum, 1)

            def terms(ps, s, a, ks, nrm=None, start=True, stop=True):
                for k in ks:
                    if nrm is not None:
                        pe.wait_ge(h_split, h_count(nrm, k))
                    c = slice(k * P, (k + 1) * P)
                    last = three(ps[:, :], w_hi[s][:, c], w_lo[s][:, c], h_hi[:, k, tok(a)], h_lo[:, k, tok(a)],
                                 start and k == ks[0], stop and k == ks[-1])
                return last

            def eight(ps, s, a, nrm=None):
                return terms(ps, s, a, range(KT), nrm)

            def ffn(ph, s0):
                per = 3 * GF

                def gate(g, i, nrm=None):
                    a, f = i // GF, i % GF
                    if nrm is None:
                        pe.wait_ge(h_split, h_count(4 * ph + a, KT - 1))
                    if i >= 2:
                        pe.wait_ge(product_made, g * (2 * GF) + (ph * GU + i - 1))
                    pe.wait_ge(unit_split, g * per + (s0 + 2 * f + 1))
                    eight(gate_bank[i % 2], 2 * f, a, nrm).then_inc(gate_made, 1)

                def up(g, i, between=None):
                    a, f = i // GF, i % GF
                    pe.wait_ge(unit_split, g * per + (s0 + 2 * f + 2))
                    ps, s = up_bank[i % 2], 2 * f + 1
                    terms(ps, s, a, range(KT // 2), stop=False)
                    if between is not None:
                        norm_sum(between)
                    terms(ps, s, a, range(KT // 2, KT), start=False).then_inc(up_made, 1)

                def gate_up(g, i, nrm=None):
                    gate(g, i, nrm)
                    up(g, i)

                def down_tiles(g, a, tiles, fs, banks=down_bank):
                    for d in tiles:
                        r = a * KT + d
                        i = d if banks is last_bank else r
                        ps = banks[i % len(banks)]
                        if i >= len(banks) and fs[0] == 0:
                            pe.wait_ge(res_added, g * (2 * KT) + (ph * (RES_FFN + RES_MIX) + r - len(banks) + 1))
                        c = slice(d * P, (d + 1) * P)
                        for f in fs:
                            last = three(ps[:, :], w_hi[DN_SLOT + f][:, c], w_lo[DN_SLOT + f][:, c],
                                         act_hi[:, f, tok(a)], act_lo[:, f, tok(a)], f == 0, f == GF - 1)
                        if fs[-1] == GF - 1:
                            last.then_inc(down_made, 1)

                def down(g, a):
                    pe.wait_ge(act_split, g * (2 * GF) + (ph * GU + GF * (a + 1)))
                    pe.wait_ge(unit_split, g * per + (s0 + per))
                    down_tiles(g, a, range(KT), range(GF))

                if ph == 0:
                    pe.wait_ge(band_copied, N_Q_HEADS)
                    pe.wait_ge(e_square, 2 * KT - 1)
                else:
                    pe.wait_ge(res_added, RES_FFN + RES_MIX - 1)
                gate(0, 0, nrm=4 * ph)
                up(0, 0, between=4 * ph + 1)
                if ph == 0:
                    pe.wait_ge(e_square, 2 * KT)
                gate_up(0, 1)
                gate_up(0, 2, nrm=4 * ph + 1)
                if ph == 0:
                    e_sums(0)
                gate_up(0, 3)
                if ph == 0:
                    e_sums(1)
                for a in (0, 1):
                    down(0, a)
                with pe.Fori(1, GROUPS - 1) as g:
                    for i in range(2 * GF):
                        gate_up(g, i)
                    for a in (0, 1):
                        down(g, a)
                g = GROUPS - 1
                gate_up(g, 0)
                gate_up(g, 1)
                gate(g, 2)
                down(g, 0)
                up(g, 2)
                norm_sum(4 * ph + 2)
                gate_up(g, 3)
                assert GF == 2
                pe.wait_ge(act_split, (ph + 1) * GU - 1)
                down_tiles(g, 1, range(4), (0,), last_bank)
                pe.wait_ge(product_made, (ph + 1) * GU)
                down_tiles(g, 1, (4,), (0,), last_bank)
                pe.wait_ge(act_split, (ph + 1) * GU)
                down_tiles(g, 1, range(5), (1,), last_bank)
                down_tiles(g, 1, range(5, KT), range(GF), last_bank)

            pe.wait_ge(oh_in, 16)
            for h in range(N_Q_HEADS):
                pe.wait_ge(rel_spread, h + 1)
                if h >= len(band_bank):
                    pe.wait_ge(band_copied, h - len(band_bank) + 1)
                pe.matmul(band_bank[h % len(band_bank)][:, 0:SKEW], relb[:, h, :], oh_sb[:, :], start=True, stop=True).then_inc(band_made, 1)

            for a in (0, 1):
                pe.wait_ge(p_split, a + 1)
                for d in range(KT):
                    n = a * KT + d
                    pe.wait_ge(unit_split, S_PROJ + d // 4 + 1)
                    wait_main_bank(n)
                    s, j = DN_SLOT + d // 4, d % 4
                    for k in range(PT_TILES):
                        c = slice((j * PT_TILES + k) * P, (j * PT_TILES + k + 1) * P)
                        last = three(main_bank[n % 2][:, :], w_hi[s][:, c], w_lo[s][:, c],
                                     act_hi[:, k, tok(a)], act_lo[:, k, tok(a)], k == 0, k == PT_TILES - 1)
                    last.then_inc(main_made, 1)
                    if n == 1:
                        pe.wait_ge(const_in, 16)
                        norm_sum(0)
            ffn(0, S_FFN1)

            def pv(u):
                b = u // 2
                pe.wait_ge(probsT_split, u + 1)
                pe.wait_ge(v_split, b // HB + 1)
                if u:
                    pe.wait_ge(attn_split, u)
                kbs = (1,) if b == 0 else (0, 1)
                for kb in kbs:
                    vb = b - 1 + kb
                    last = three(pv_bank[:, :], v_hi[:, vb, :], v_lo[vb // HB][:, vb % HB, :],
                                 probsT_hi[:, kb, :], probsT_lo[kb][:, :], kb == kbs[0], kb == 1)
                last.then_inc(pv_made, 1)

            pe.wait_ge(product_made, GU)
            seen = set()
            for step in PLAN:
                kind = step[0]
                if kind == "win":
                    n, m, a = MAIN_AT[step], MIXU_AT[step], step[1]
                    if n >= 2 * KT + 2:
                        wait_main_bank(n)
                    pe.wait_ge(unit_split, S_MIX + m + 1)
                    eight(main_bank[n % 2], m % MIX_SLOTS, a, None if a in seen else 2 + a).then_inc(main_made, 1)
                    seen.add(a)
                elif kind == "norm":
                    if step[1] == 3:
                        norm_sum(3)
                elif kind == "qks":
                    i = QKS_AT[step[1:]]
                    pe.wait_ge(qk_square, i + 1)
                    wait_sum_bank(step)
                    pe.matmul(sum_bank[:, :], blockones, qb[i % 2][:, :], start=True, stop=True).then_inc(qk_sum, 1)
                elif kind == "vt":
                    pe.wait_ge(main_copied, copied(("win", step[1], "v", 0)))
                    wait_sum_bank(step)
                    for j in range(HB):
                        c = slice(j * P, (j + 1) * P)
                        last = pe.transpose(sum_bank[:, c], vT[:, c], ident)
                    last.then_inc(v_turned, 1)
                elif kind == "scores":
                    u = step[1]
                    b, kv = u // 2, u % 2
                    p0, off = kv * HEAD_DIM, (P if b == 0 else 0)
                    if u == 0:
                        pe.wait_ge(res_added, RES_FFN)
                    pe.wait_ge(qk_normed, QKS_AT[(b // HB, "q", HPK - 1)] + 1)
                    if u:
                        pe.wait_ge(scores_biased, HPK * u)
                    for h in range(HPK):
                        c = (h % 2) * 2 * P
                        last = pe.matmul(score_bank[h // 2][:, c + off:c + 2 * P],
                                         q_sb[p0:p0 + HEAD_DIM, h, b * P:(b + 1) * P],
                                         k_sb[p0:p0 + HEAD_DIM, max(b - 1, 0) * P:(b + 1) * P], start=True, stop=True)
                    last.then_inc(scores_made, 1)
                elif kind == "probs":
                    u = step[1]
                    pe.wait_ge(probs_normed, HPK * (u + 1))
                    if u:
                        pe.wait_ge(probsT_split, u)
                    for kb in ((1,) if u < 2 else (0, 1)):
                        for h in range(HPK):
                            last = pe.transpose(probsT_bank[kb][:, h * P:(h + 1) * P],
                                                probs[:, h, kb * P:(kb + 1) * P], ident)
                    last.then_inc(probs_turned, 1)
                elif kind == "pv":
                    if step[1] < 2 * NB - 1:
                        pv(step[1])
                elif kind == "pool":
                    n, g = MAIN_AT[step], step[2]
                    wait_main_bank(n)
                    pe.wait_ge(pool_in, POOLS.index(step[1:]) + 1)
                    c = slice(g * P, (g + 1) * P)
                    three(main_bank[n % 2][:, :], pw_hi[:, c], pw_lo[:, c], d_hi[:, :], d_lo[:, :],
                          True, True).then_inc(main_made, 1)
                elif kind == "wouts":
                    pe.wait_ge(pool_split, NG * 2)
                    for d in (0, 1):
                        wout = ("wout", 1, d)
                        n, m = MAIN_AT[wout], MIXU_AT[wout]
                        wait_main_bank(n)
                        pe.wait_ge(unit_split, S_MIX + m + 1)
                        terms(main_bank[n % 2], m % MIX_SLOTS, 1, range(HPK, KT), stop=False)
                        if d == 0:
                            pv(2 * NB - 1)
                    norm_sum(4)
                elif kind == "wout":
                    n, m, a = MAIN_AT[step], MIXU_AT[step], step[1]
                    pe.wait_ge(attn_split, NB * (a + 1))
                    if a and step[2] < 2:
                        terms(main_bank[n % 2], m % MIX_SLOTS, a, range(HPK), start=False).then_inc(main_made, 1)
                        continue
                    wait_main_bank(n)
                    pe.wait_ge(unit_split, S_MIX + m + 1)
                    pe.wait_ge(pool_split, NG * (a + 1))
                    eight(main_bank[n % 2], m % MIX_SLOTS, a).then_inc(main_made, 1)

            ffn(1, S_FFN2)

            pe.wait_ge(product_made, 2 * GU)
            for a in (0, 1):
                for d in range(KT):
                    n, m = MAIN_AT[("gate", a, d)], a * KT + d
                    if m >= 2:
                        wait_main_bank(n)
                    pe.wait_ge(unit_split, S_GATE + m + 1)
                    eight(main_bank[n % 2], m % MIX_SLOTS, a, 6 + a if d == 0 else None).then_inc(main_made, 1)
                    if m == 2:
                        norm_sum(7)

        @block.scalar
        def _(act):
            def square(nrm, k, src):
                dst = acc[nrm % 2] if k == 0 else sq[k % 2]
                if k == 0:
                    if nrm >= 2:
                        act.wait_ge(sum_made, nrm - 1)
                elif k <= 2:
                    if nrm >= 1:
                        act.wait_ge(squares_added, acc_count(nrm, 0))
                else:
                    act.wait_ge(squares_added, acc_count(nrm, k - 2))
                act.activation(dst[:, :], src, ACT.Square).then_inc(square_made, 1)

            def std(nrm):
                act.wait_ge(sum_made, nrm + 1)
                if nrm >= 2:
                    act.wait_ge(h_normed, h_count(nrm - 2, KT - 1))
                act.activation(rstd[nrm % 2][:, :], sum_bank[:, :], ACT.Sqrt, bias=col(C_EPS),
                               scale=1.0 / D_MODEL).then_inc(std_made, 1)

            def round_h(nrm, k):
                act.wait_ge(h_normed, h_count(nrm, k))
                act.activation(h_hi[:, k, tok(nrm % 2)], hn[k % 2][:, :], ACT.Copy).then_inc(h_rounded, 1)

            def ffn(ph):
                def silu_tile(g, i):
                    act.wait_ge(gate_made, g * (2 * GF) + (ph * GU + i + 1))
                    act.activation(silu[i % 2][:, :], gate_bank[i % 2][:, :], ACT.Silu).then_inc(silu_made, 1)

                def round_tile(g, i):
                    act.wait_ge(product_made, g * (2 * GF) + (ph * GU + i + 1))
                    act.activation(act_hi[:, i % GF, tok(i // GF)], prod[i % 2][:, :], ACT.Copy).then_inc(act_rounded, 1)

                if ph == 0:
                    for k in range(KT):
                        act.wait_ge(x_in[2 + k // (KT // 2)], 16)
                        square(1, k, x_sb[:, k, tok(1)])
                    for i in range(4):
                        act.wait_ge(e_out[i], 16 * (2 * KT // 4))
                silu_tile(0, 0)
                std(4 * ph + 1)
                if ph == 0:
                    act.wait_ge(band_out, 16 * N_Q_HEADS)
                for k in range(KT):
                    if k == 2:
                        round_tile(0, 0)
                    round_h(4 * ph + 1, k)
                for i in (1, 2):
                    silu_tile(0, i)
                    round_tile(0, i)
                if ph == 0:
                    e_root(0)
                silu_tile(0, 3)
                round_tile(0, 3)
                if ph == 0:
                    e_root(1)
                    act.wait_ge(e_added[0], KT - 1)
                    act.wait_ge(e_added[1], KT - 1)
                    skewed = bass.AP(tensor=band.tensor, offset=P - 1, ap=[[SKEW - 1, P], [P * SKEW, N_Q_HEADS], [1, 2 * P]])
                    act.dma_start(bias[:, :, :], skewed).then_inc(bias_in, 16)
                    for a in (0, 1):
                        act.wait_ge(e_rstd, a + 1)
                        act.dma_start(e_dram[a, :, KT, :], eacc[a][:, :]).then_inc(re_out[a], 16)
                with act.Fori(1, GROUPS - 1) as g:
                    for i in range(2 * GF):
                        silu_tile(g, i)
                        round_tile(g, i)
                g = GROUPS - 1
                r0 = ph * (RES_FFN + RES_MIX) + 2 * KT * g
                for i in range(2):
                    silu_tile(g, i)
                    round_tile(g, i)
                silu_tile(g, 2)
                for k in range(KT):
                    act.wait_ge(res_added, r0 + k + 1)
                    square(4 * ph + 2, k, x_sb[:, k, tok(0)])
                round_tile(g, 2)
                std(4 * ph + 2)
                for k in range(EARLY):
                    round_h(4 * ph + 2, k)
                silu_tile(g, 3)
                round_tile(g, 3)
                for k in range(KT):
                    if EARLY + k < KT:
                        round_h(4 * ph + 2, EARLY + k)
                    act.wait_ge(res_added, r0 + KT + k + 1)
                    square(4 * ph + 3, k, x_sb[:, k, tok(1)])

            act.dma_start(small_sb[:, :], small).then_inc(small_in, 16)
            def load_x(i):
                a, k = i // 2, (i % 2) * (KT // 2)
                act.dma_start(x_sb[:, k:k + KT // 2, tok(a)],
                              xT[k * P:(k + KT // 2) * P, tok(a)].rearrange("(k p) t -> p k t", p=P)).then_inc(x_in[i], 16)

            load_x(0)
            act.dma_start(const_sb[:, :], const).then_inc(const_in, 16)
            load_x(1)

            for h in range(N_Q_HEADS):
                act.wait_ge(band_made, h + 1)
                act.activation(gband[h][:, :], band_bank[h % 4][:, 0:SKEW], ACT.Copy).then_inc(band_copied, 1)
                act.wait_ge(x_in[h // (KT // 2)], 16)
                square(0, h, x_sb[:, h, tok(0)])

            def e_root(a):
                act.wait_ge(e_sum, a + 1)
                act.activation(eacc[a][:, :], sum_bank[:, :], ACT.Sqrt, bias=col(C_EPS), scale=1.0 / D_MODEL).then_inc(e_std, 1)

            def e_tile(n):
                a, d = n // KT, n % KT
                act.wait_ge(main_made, n + 1)
                if n >= 4:
                    act.wait_ge(e_out[n % 4], 16 * (n // 4))
                act.activation(et[n % 4][:, :], main_bank[n % 2][:, :], ACT.Copy).then_inc(e_copied, 1)
                if d > 4:
                    act.wait_ge(e_added[a], d - 4)
                elif d and a:
                    act.wait_ge(e_added[0], KT - 1)
                elif d:
                    act.wait_ge(p_split, 2)
                dst = eacc[a] if d == 0 else esq[d % 4]
                act.activation(dst[:, :], main_bank[n % 2][:, :], ACT.Square).then_inc(e_square, 1)
                act.wait_ge(e_copied, n + 1)
                act.dma_start(e_dram[a, :, d, :], et[n % 4][:, :]).then_inc(e_out[n % 4], 16)

            act.wait_ge(small_in, 16)
            for n in range(2 * KT):
                e_tile(n)
                if n == 1:
                    std(0)
                if n in (4, 7):
                    load_x(2 + (n > 4))
                if LAG <= n < LAG + KT:
                    round_h(0, n - LAG)
            ffn(0)

            for a in (0, 1):
                act.wait_ge(re_out[a], 16)
            for step in PLAN:
                kind = step[0]
                if kind == "win":
                    n, a, what, i = MAIN_AT[step], *step[1:]
                    ps = main_bank[n % 2][:, :]
                    act.wait_ge(main_made, n + 1)
                    if what == "v":
                        if a:
                            act.wait_ge(v_turned, a)
                        act.activation(vT[:, :], ps, ACT.Copy).then_inc(main_copied, 1)
                    elif what == "u":
                        if a:
                            act.wait_ge(pool_in, i + 1)
                        act.activation(ub[:, i, HALO:UB], ps, ACT.Copy).then_inc(main_copied, 1)
                    else:
                        dst = k_sb[:, tok(a)] if what == "k" else q_sb[:, i, tok(a)]
                        j = QKS_AT[(a, what, i)]
                        act.activation(dst, ps, ACT.Copy).then_inc(main_copied, 1)
                        act.wait_ge(main_copied, copied(step))
                        if j >= 2:
                            act.wait_ge(qk_normed, j - 1)
                        act.activation(qb[j % 2][:, :], dst, ACT.Square).then_inc(qk_square, 1)
                elif kind == "qks":
                    i, q = QKS_AT[step[1:]], step[2] == "q"
                    act.wait_ge(qk_sum, i + 1)
                    act.activation(qb[i % 2][:, :], sum_bank[:, :], ACT.Sqrt, bias=col(C_EPSQ if q else C_EPS),
                                   scale=1.0 if q else 1.0 / HEAD_DIM).then_inc(qk_std, 1)
                elif kind == "vt":
                    a = step[1]
                    act.wait_ge(v_turned, a + 1)
                    act.activation(v_hi[:, a * HB:(a + 1) * HB, :], sum_bank[:, :].rearrange("p (b c) -> p b c", b=HB),
                                   ACT.Copy).then_inc(v_rounded, 1)
                elif kind == "norm":
                    std(step[1])
                elif kind == "tile":
                    if step[2] < KT:
                        round_h(*step[1:])
                elif kind == "scores":
                    u = step[1]
                    off = P if u < 2 else 0
                    act.wait_ge(max_made, u + 1)
                    act.activation(stats[:, ES, :], stats[:, SM, :], ACT.Exp)
                    for h in range(HPK):
                        last = act.activation(probs[:, h, off:], probs[:, h, off:], ACT.Exp, bias=stats[:, NEGM, h:h + 1],
                                              accum_out=stats[:, DEN, h:h + 1])
                    last.then_inc(exp_made, 1)
                elif kind == "probs":
                    u = step[1]
                    act.wait_ge(probs_turned, u + 1)
                    if u:
                        act.wait_ge(pv_made, u)
                    for kb in ((1,) if u < 2 else (0, 1)):
                        last = act.activation(probsT_hi[:, kb, :], probsT_bank[kb][:, :], ACT.Copy)
                    last.then_inc(probsT_rounded, 1)
                elif kind == "pv":
                    u = step[1]
                    b, p0 = u // 2, (u % 2) * HEAD_DIM
                    act.wait_ge(pv_made, u + 1)
                    act.activation(h_hi[p0:p0 + HEAD_DIM, 0:HPK, b * P:(b + 1) * P],
                                   pv_bank[p0:p0 + HEAD_DIM, :].rearrange("p (h q) -> p h q", h=HPK),
                                   ACT.Copy).then_inc(attn_rounded, 1)
                elif kind == "pool":
                    n, a, g = MAIN_AT[step], *step[1:]
                    act.wait_ge(main_made, n + 1)
                    act.activation(h_hi[:, HPK + g, tok(a)], main_bank[n % 2][:, :], ACT.Copy,
                                   scale=col(C_PSCALE + g)).then_inc(pool_rounded, 1)
                elif kind == "wout":
                    a, d = step[1:]
                    act.wait_ge(res_added, RES_FFN + a * KT + d + 1)
                    square(4 + a, d, x_sb[:, d, tok(a)])
            ffn(1)

            for a in (0, 1):
                for d in range(KT):
                    n, m = MAIN_AT[("gate", a, d)], a * KT + d
                    act.wait_ge(main_made, n + 1)
                    if m >= 2:
                        act.wait_ge(y_made, m - 1)
                    act.activation(silu[m % 2][:, :], main_bank[n % 2][:, :], ACT.Sigmoid,
                                   bias=col(C_BGATE + d)).then_inc(sig_made, 1)
                    if m == 2:
                        std(7)
                    for k in range(max(0, 2 * m - 4), min(2 * m - 2, KT)):
                        round_h(7, k)

        @block.vector
        def _(dve):
            steps = [0]

            def link(ins):
                steps[0] += 1
                ins.then_inc(dve_step, 1)
                dve.wait_ge(dve_step, steps[0])

            def accumulate(nrm, k):
                dve.wait_ge(square_made, sq_count(nrm, k))
                if k >= 2:
                    dve.wait_ge(squares_added, acc_count(nrm, k - 1))
                a = acc[nrm % 2][:, :]
                dve.tensor_tensor(a, a, sq[k % 2][:, :], ALU.add).then_inc(squares_added, 1)

            def reciprocal(nrm):
                r = rstd[nrm % 2][:, :]
                dve.wait_ge(std_made, nrm + 1)
                dve.reciprocal(r, r).then_inc(rstd_made, 1)
                dve.wait_ge(rstd_made, nrm + 1)

            def norm_tile(nrm, k):
                if h_count(nrm, k) > 2:
                    dve.wait_ge(h_split, h_count(nrm, k) - 2)
                g = C_GAIN[nrm // 2] + k
                dve.scalar_tensor_tensor(hn[k % 2][:, :], x_sb[:, k, tok(nrm % 2)], col(g), rstd[nrm % 2][:, :],
                                         ALU.mult, ALU.mult).then_inc(h_normed, 1)

            def split_tile(nrm, k):
                dve.wait_ge(h_rounded, h_count(nrm, k))
                a = tok(nrm % 2)
                dve.tensor_tensor(h_lo[:, k, a], hn[k % 2][:, :], plain(h_hi[:, k, a]), ALU.subtract).then_inc(h_split, 1)

            def tile(nrm, k):
                if k < KT:
                    norm_tile(nrm, k)
                if k:
                    split_tile(nrm, k - 1)

            def e_reciprocal(a):
                dve.wait_ge(e_std, a + 1)
                dve.reciprocal(eacc[a][:, :], eacc[a][:, :]).then_inc(e_rstd, 1)

            def ffn(ph):
                def product(g, i):
                    t = ph * GU + i + 1
                    dve.wait_ge(up_made, g * (2 * GF) + t)
                    dve.wait_ge(silu_made, g * (2 * GF) + t)
                    if i >= 2:
                        dve.wait_ge(act_split, g * (2 * GF) + t - 2)
                    dve.tensor_tensor(prod[i % 2][:, :], silu[i % 2][:, :], up_bank[i % 2][:, :], ALU.mult).then_inc(product_made, 1)
                    dve.wait_ge(act_rounded, g * (2 * GF) + t)
                    f, a = i % GF, tok(i // GF)
                    dve.tensor_tensor(act_lo[:, f, a], prod[i % 2][:, :], plain(act_hi[:, f, a]), ALU.subtract).then_inc(act_split, 1)

                def residual(g, r, ps=None):
                    ps = ps or down_bank[r % 3]
                    dve.wait_ge(down_made, g * (2 * KT) + (ph * RES_FFN + r + 1))
                    x = x_sb[:, r % KT, tok(r // KT)]
                    dve.scalar_tensor_tensor(x, ps[:, :], MACARON_WEIGHT, x, ALU.mult, ALU.add).then_inc(res_added, 1)

                for k in range(1 if ph == 0 else KT - 1, KT):
                    accumulate(4 * ph + 1, k)
                reciprocal(4 * ph + 1)
                for k in range(KT + 1):
                    if k == 2:
                        product(0, 0)
                    tile(4 * ph + 1, k)
                for i in (1, 2):
                    product(0, i)
                if ph == 0:
                    e_reciprocal(0)
                product(0, 3)
                for r in range(2 * KT):
                    residual(0, r)
                if ph == 0:
                    e_reciprocal(1)
                with dve.Fori(1, GROUPS - 1) as g:
                    for i in range(2 * GF):
                        product(g, i)
                    for r in range(2 * KT):
                        residual(g, r)
                g, na = GROUPS - 1, 4 * ph + 2
                for i in range(2):
                    product(g, i)
                for k in range(KT):
                    residual(g, k)
                    if k >= 2:
                        accumulate(na, k - 1)
                accumulate(na, KT - 1)
                product(g, 2)
                reciprocal(na)
                for k in range(EARLY):
                    tile(na, k)
                product(g, 3)
                for k in range(KT):
                    residual(g, KT + k, last_bank[k % len(last_bank)])
                    if EARLY + k <= KT:
                        tile(na, EARLY + k)

            dve.memset(rel_sb[N_BUCKETS:N_BUCKETS + 1, :], 1.0).then_inc(rel_one, 1)
            dve.memset(relb[:, :, :], 1.0).then_inc(rel_one, 1)
            dve.wait_ge(rel_one, 2)
            dve.wait_ge(rel_in, 16)
            for h in range(N_Q_HEADS):
                dve.tensor_scalar(relb[:, h, :], relb[:, h, :], rel_sb[:, h:h + 1], None, ALU.mult).then_inc(rel_spread, 1)

            def split_p(a):
                hi, p_half = act_hi[:, :, tok(a)], p_raw[:, :, tok(a)]
                dve.wait_ge(p_in[a], 16)
                dve.tensor_copy(hi, p_half).then_inc(p_rounded, 1)
                dve.wait_ge(p_rounded, a + 1)
                dve.tensor_tensor(act_lo[:, :, tok(a)], p_half, plain(hi), ALU.subtract).then_inc(p_split, 1)

            split_p(0)

            def e_accumulate(k):
                dve.wait_ge(e_square, k + 1)
                if k >= 2:
                    dve.wait_ge(e_added[0], k - 1)
                dve.tensor_tensor(eacc[0][:, :], eacc[0][:, :], esq[k % 4][:, :], ALU.add).then_inc(e_added[0], 1)

            dve.wait_ge(small_in, 16)
            for k in range(1, KT):
                accumulate(0, k)
                if k == KT // 2:
                    split_p(1)
            e_accumulate(1)
            reciprocal(0)
            e_accumulate(2)
            e_accumulate(3)
            for k in range(KT + 1):
                tile(0, k)
                if k < 4:
                    e_accumulate(k + 4)
            ffn(0)

            def split_probs(u):
                dve.wait_ge(probsT_rounded, u + 1)
                for kb in ((1,) if u < 2 else (0, 1)):
                    last = dve.tensor_tensor(probsT_lo[kb][:, :], probsT_bank[kb][:, :], plain(probsT_hi[:, kb, :]), ALU.subtract)
                last.then_inc(probsT_split, 1)

            dve.wait_ge(bias_in, 16)
            for step in PLAN:
                kind = step[0]
                if kind == "norm":
                    nrm = step[1]
                    if nrm > 3:
                        accumulate(nrm, KT - 1)
                    reciprocal(nrm)
                elif kind == "tile":
                    tile(*step[1:])
                elif kind == "qks":
                    a, what, i = step[1:]
                    j = QKS_AT[step[1:]]
                    dve.wait_ge(qk_std, j + 1)
                    link(dve.reciprocal(qb[j % 2][:, :], qb[j % 2][:, :]))
                    t = k_sb[:, tok(a)] if what == "k" else q_sb[:, i, tok(a)]
                    dve.scalar_tensor_tensor(t, t, col(C_KN if what == "k" else C_QN), qb[j % 2][:, :],
                                             ALU.mult, ALU.mult).then_inc(qk_normed, 1)
                elif kind == "scores":
                    u = step[1]
                    kv, off = u % 2, (P if u < 2 else 0)
                    dve.wait_ge(scores_made, u + 1)
                    for h in range(HPK):
                        c = (h % 2) * 2 * P
                        hh = kv * HPK + h
                        dve.tensor_tensor_reduce(probs[:, h, off:], score_bank[h // 2][:, c + off:c + 2 * P],
                                                 bias[:, hh, off:], 1.0, col(C_SINK + hh), ALU.add, ALU.max,
                                                 stats[:, MX, h:h + 1]).then_inc(scores_biased, 1)
                    dve.wait_ge(scores_biased, HPK * (u + 1))
                    link(dve.tensor_scalar(stats[:, NEGM, :], stats[:, MX, :], -1.0, None, ALU.mult))
                    c = C_SINK + kv * HPK
                    dve.tensor_tensor(stats[:, SM, :], stats[:, NEGM, :], small_sb[:, c:c + HPK], ALU.add).then_inc(max_made, 1)
                    if u % NB:
                        split_probs(u - 1)
                    dve.wait_ge(exp_made, u + 1)
                    link(dve.tensor_tensor(stats[:, RCP, :], stats[:, DEN, :], stats[:, ES, :], ALU.add))
                    link(dve.reciprocal(stats[:, RCP, :], stats[:, RCP, :]))
                    for h in range(HPK):
                        dve.tensor_scalar(probs[:, h, off:], probs[:, h, off:], stats[:, RCP, h:h + 1], None,
                                          ALU.mult).then_inc(probs_normed, 1)
                elif kind == "vt":
                    a = step[1]
                    dve.wait_ge(v_rounded, a + 1)
                    dve.tensor_tensor(v_lo[a][:, :, :], sum_bank[:, :].rearrange("p (b c) -> p b c", b=HB),
                                      plain(v_hi[:, a * HB:(a + 1) * HB, :]), ALU.subtract).then_inc(v_split, 1)
                elif kind == "pv":
                    u = step[1]
                    b, p0 = u // 2, (u % 2) * HEAD_DIM
                    if u % NB == NB - 1:
                        split_probs(u)
                    at = (slice(p0, p0 + HEAD_DIM), slice(0, HPK), slice(b * P, (b + 1) * P))
                    dve.wait_ge(attn_rounded, u + 1)
                    dve.tensor_tensor(h_lo[at], pv_bank[p0:p0 + HEAD_DIM, :].rearrange("p (h q) -> p h q", h=HPK),
                                      plain(h_hi[at]), ALU.subtract).then_inc(attn_split, 1)
                elif kind == "pool":
                    n, a, g = MAIN_AT[step], *step[1:]
                    dve.wait_ge(pool_rounded, POOLS.index((a, g)) + 1)
                    dve.scalar_tensor_tensor(h_lo[:, HPK + g, tok(a)], main_bank[n % 2][:, :], col(C_PSCALE + g),
                                             plain(h_hi[:, HPK + g, tok(a)]), ALU.mult, ALU.subtract).then_inc(pool_split, 1)
                elif kind == "wout":
                    n, a, d = MAIN_AT[step], *step[1:]
                    if d == 0:
                        dve.wait_ge(res_added, RES_FFN + a * KT)
                    dve.wait_ge(main_made, n + 1)
                    x = x_sb[:, d, tok(a)]
                    dve.tensor_tensor(x, x, main_bank[n % 2][:, :], ALU.add).then_inc(res_added, 1)
                    if d >= 2:
                        accumulate(4 + a, d - 1)
            ffn(1)

            def finish(m):
                a, d = m // KT, m % KT
                e = e_sb[a][:, d, :]
                x = x_sb[:, d, tok(a)]
                dve.wait_ge(e_in[a], 32)
                link(dve.scalar_tensor_tensor(e, e, col(C_G["post"] + d), re_sb[:, a, :], ALU.mult, ALU.mult))
                dve.wait_ge(sig_made, m + 1)
                link(dve.tensor_tensor(e, e, silu[m % 2][:, :], ALU.mult))
                dve.tensor_tensor(x, x, e, ALU.add).then_inc(y_made, 1)

            for m in range(2 * KT):
                finish(m)
                if m == 2:
                    reciprocal(7)
                for k in range(max(0, 2 * m - 4), min(2 * m - 2, KT + 1)):
                    tile(7, k)


def build(nc, xT, pT, units, poolw, small, const, onehot, rel, out):
    band = nc.dram_tensor("band", (N_Q_HEADS, P, SKEW), F32, kind="Internal").ap()
    e_dram = nc.dram_tensor("e_dram", (2, P, KT + 1, HALF), F32, kind="Internal").ap()
    program(nc, xT, pT, units, poolw, small, const, onehot, rel, band, e_dram, out)


def constants():
    c = np.zeros((P, N_CONST), np.float32)
    c[:, K_ID:K_ID + P] = np.eye(P)
    c[:, K_ONES:K_ONES + P] = 1.0
    c[:, K_BLK:K_BLK + P] = np.kron(np.eye(P // HEAD_DIM), np.ones((HEAD_DIM, HEAD_DIM)))
    for g, w in enumerate(POOL_WINDOWS):
        c[:, K_RC + g * HALO:K_RC + (g + 1) * HALO] = 1.0 / np.minimum(np.arange(HALO) + 1, w)
    return c


def onehots():
    oh = np.zeros((N_BUCKETS + 1, SKEW), np.float32)
    half = N_BUCKETS // 2
    for i in range(SKEW):
        n = 2 * P - 1 - i
        if 0 <= n < WINDOW:
            b = n if n < half else min(N_BUCKETS - 1, half + int(
                math.log(n / half) / math.log(MAX_DISTANCE / half) * (N_BUCKETS - half) + 1e-9))
            oh[b, i] = 1.0
        else:
            oh[N_BUCKETS, i] = NEG_INF
    return oh


def pack_ffn(w_gu, w_down):
    gu = w_gu.reshape(KT, P, 2, GROUPS, GF, P).transpose(3, 4, 2, 1, 0, 5).reshape(GROUPS, 2 * GF, P, UNIT)
    dn = w_down.reshape(GROUPS, GF, P, D_MODEL)
    return np.concatenate([gu, dn], axis=1).reshape(FFN_UNITS, P, UNIT)


def pack_square(w):
    n = w.shape[1] // P
    return w.reshape(KT, P, n, P).transpose(2, 1, 0, 3).reshape(n, P, UNIT)


def kernel(x, p, ffn1_norm, ffn1_w_gu, ffn1_w_down, mix_norm, w_in, q_norm, k_norm,
           rel_bias, sinks, pool_w, pool_scale, w_out, ffn2_norm, ffn2_w_gu, ffn2_w_down,
           ple_norm, ple_w_gate, ple_b_gate, ple_w_proj, ple_post_norm):
    import concourse.bacc as bacc
    from concourse.bass_utils import run_bass_kernel_spmd

    f = np.ascontiguousarray
    heads = np.arange(ATTN_WIDTH).reshape(N_KV_HEADS, HPK, HEAD_DIM).transpose(1, 0, 2).reshape(-1)
    w_in = np.asarray(w_in)[0]
    w_in = np.concatenate([w_in[:, heads], w_in[:, ATTN_WIDTH:]], axis=1)
    w_out = np.asarray(w_out)[0]
    w_out = np.concatenate([w_out[heads], w_out[ATTN_WIDTH:]], axis=0)
    proj = np.asarray(ple_w_proj)[0].reshape(PT_TILES, P, 2, KT // 2, P).transpose(2, 1, 3, 0, 4).reshape(2, P, UNIT)
    units = np.concatenate([
        proj, pack_ffn(np.asarray(ffn1_w_gu)[0], np.asarray(ffn1_w_down)[0]), pack_square(w_in), pack_square(w_out),
        pack_ffn(np.asarray(ffn2_w_gu)[0], np.asarray(ffn2_w_down)[0]), pack_square(np.asarray(ple_w_gate)[0])])

    def by_partition(v):
        return np.asarray(v)[0].reshape(-1, P).T

    def twice(v):
        return np.tile(np.asarray(v)[0], P // HEAD_DIM)[:, None]

    eps = np.zeros((P, 2), np.float32)
    eps[:, 0], eps[:, 1] = EPS, EPS * HEAD_DIM
    small = np.concatenate([
        by_partition(ffn1_norm), by_partition(mix_norm), by_partition(ffn2_norm), by_partition(ple_norm),
        by_partition(ple_post_norm), by_partition(ple_b_gate), by_partition(pool_scale), twice(q_norm), twice(k_norm),
        np.broadcast_to(np.asarray(sinks), (P, N_Q_HEADS)), eps], axis=1)
    arrays = {
        "xT": f(np.asarray(x)[0].T), "pT": f(np.asarray(p)[0, 0].T), "units": f(units),
        "poolw": f(np.asarray(pool_w)[0].transpose(1, 0, 2).reshape(P, NG * P)), "small": f(small),
        "const": constants(), "onehot": onehots(), "rel": f(np.asarray(rel_bias)),
    }
    nc = bacc.Bacc("TRN2", target_bir_lowering=False, num_devices=1, dynamic_dma_scratch_size=1024)
    args = [nc.dram_tensor(f"in_{k}", v.shape, mybir.dt.from_np(v.dtype), kind="ExternalInput").ap()
            for k, v in arrays.items()]
    out = nc.dram_tensor("outT", (D_MODEL, SEQ), F32, kind="ExternalOutput").ap()
    build(nc, *args, out)
    r = run_bass_kernel_spmd(nc, [{f"in_{k}": v for k, v in arrays.items()}], core_ids=[0])
    return f(r.results[0]["outT"].T)[None]
```
